# Optimizing a Trainium2 kernel written in Bass

```python
import jax, jax.numpy as jnp
from jax import lax
import numpy as np

D_MODEL = 1024
BATCH = 1
SEQ = 512
DEPTH = 1

N_HEADS = 8
N_KV = 2
GQ = N_HEADS // N_KV
HD = 64
Q_WIDTH = N_HEADS * HD
KV_WIDTH = N_KV * HD
WINDOW = 128
BLK = 128
N_FGROUPS = 4
FG_DIM = 128
F_WIDTH = N_FGROUPS * FG_DIM
N_BUCKETS = 32
MAX_DIST = 128
D_FF = 2816
EPS = 1e-6
NEG = -1e30
IN_WIDTH = Q_WIDTH + 2 * KV_WIDTH + F_WIDTH + 2 * D_MODEL

kernel_name = "hybrid_window_gqa_fnet_gated_macaron"

def _rms(x, g):
    xf = x.astype(jnp.float32)
    y = xf * lax.rsqrt(jnp.mean(xf * xf, axis=-1, keepdims=True) + EPS)
    return (y * g.astype(jnp.float32)).astype(x.dtype)

def _swiglu(h, w_up, w_down):
    gate, up = jnp.split(h @ w_up, 2, axis=-1)
    return (jax.nn.silu(gate) * up) @ w_down

def _t5_bucket_and_rel():
    rel = (np.arange(3 * BLK)[None, :] - BLK) - np.arange(BLK)[:, None]
    half = N_BUCKETS // 2
    max_exact = half // 2
    ret = (rel > 0).astype(np.int32) * half
    n = np.abs(rel)
    n_safe = np.maximum(n, 1).astype(np.float32)
    large = max_exact + (np.log(n_safe / max_exact) / np.log(MAX_DIST / max_exact)
                         * (half - max_exact)).astype(np.int32)
    large = np.minimum(large, half - 1)
    bucket = ret + np.where(n < max_exact, n, large)
    return rel, bucket.astype(np.int32)

def _window_attention(q, k, v, sink, rel_bias):
    B, S = q.shape[0], q.shape[1]
    nb = S // BLK
    qb = q.reshape(B, nb, BLK, N_KV, GQ, HD).astype(jnp.float32)
    pad = ((0, 0), (BLK, BLK), (0, 0))
    kp = jnp.pad(k, pad).reshape(B, nb + 2, BLK, N_KV, HD)
    vp = jnp.pad(v, pad).reshape(B, nb + 2, BLK, N_KV, HD)

    def win(t):
        return jnp.concatenate([t[:, :-2], t[:, 1:-1], t[:, 2:]], axis=2).astype(jnp.float32)

    kw, vw = win(kp), win(vp)
    s = jnp.einsum('bnqkgd,bnjkd->bnkgqj', qb, kw) * (HD ** -0.5)

    rel, bucket = _t5_bucket_and_rel()
    bias = rel_bias.astype(jnp.float32)[bucket]
    bias = jnp.transpose(bias, (2, 0, 1)).reshape(N_KV, GQ, BLK, 3 * BLK)
    key_idx = np.arange(nb)[:, None] * BLK - BLK + np.arange(3 * BLK)[None, :]
    mask = (np.abs(rel) <= WINDOW)[None] & ((key_idx >= 0) & (key_idx < S))[:, None, :]
    mask = jnp.asarray(mask)[None, :, None, None]
    s = jnp.where(mask, s + bias, NEG)

    sk = sink.astype(jnp.float32).reshape(1, 1, N_KV, GQ, 1, 1)
    m = jnp.maximum(s.max(axis=-1, keepdims=True), sk)
    p = jnp.exp(s - m)
    w = p / (p.sum(axis=-1, keepdims=True) + jnp.exp(sk - m))
    o = jnp.einsum('bnkgqj,bnjkd->bnqkgd', w, vw)
    return o.reshape(B, S, Q_WIDTH).astype(q.dtype)

def _fourier_mix(f):
    B, S = f.shape[0], f.shape[1]
    fg = f.astype(jnp.float32).reshape(B, S, N_FGROUPS, FG_DIM)
    y = jnp.fft.fft2(fg, axes=(1, 3), norm="ortho").real
    return y.reshape(B, S, F_WIDTH).astype(f.dtype)

def setup_inputs(seed: int = 0) -> dict:
    key = jax.random.key(seed)
    ks = jax.random.split(key, 20)
    f32 = jnp.float32

    def w(k, shape, fan_in):
        return jax.random.normal(k, shape, f32) * (fan_in ** -0.5)

    def gain(k, shape):
        return 1.0 + 0.02 * jax.random.normal(k, shape, f32)

    return {
        "x": jax.random.normal(ks[0], (BATCH, SEQ, D_MODEL), f32),
        "g_ffn1": gain(ks[1], (DEPTH, D_MODEL)),
        "w_up1": w(ks[2], (DEPTH, D_MODEL, 2 * D_FF), D_MODEL),
        "w_down1": w(ks[3], (DEPTH, D_FF, D_MODEL), D_FF),
        "g_mix": gain(ks[4], (DEPTH, D_MODEL)),
        "w_in": w(ks[5], (DEPTH, D_MODEL, IN_WIDTH), D_MODEL),
        "b_gate": 0.01 * jax.random.normal(ks[6], (DEPTH, 2 * D_MODEL), f32),
        "sink": 0.5 * jax.random.normal(ks[7], (DEPTH, N_HEADS), f32),
        "rel_bias": 0.5 * jax.random.normal(ks[8], (N_BUCKETS, N_HEADS), f32),
        "w_branch_a": w(ks[9], (DEPTH, Q_WIDTH, D_MODEL), Q_WIDTH),
        "w_branch_b": w(ks[10], (DEPTH, F_WIDTH, D_MODEL), F_WIDTH),
        "w_out": w(ks[11], (DEPTH, D_MODEL, D_MODEL), D_MODEL),
        "g_ffn2": gain(ks[12], (DEPTH, D_MODEL)),
        "w_up2": w(ks[13], (DEPTH, D_MODEL, 2 * D_FF), D_MODEL),
        "w_down2": w(ks[14], (DEPTH, D_FF, D_MODEL), D_FF),
        "g_final": gain(ks[15], (D_MODEL,)),
    }

def reference(x, g_ffn1, w_up1, w_down1, g_mix, w_in, b_gate, sink, rel_bias,
              w_branch_a, w_branch_b, w_out, g_ffn2, w_up2, w_down2, g_final):
    o_q = Q_WIDTH
    o_k = o_q + KV_WIDTH
    o_v = o_k + KV_WIDTH
    o_f = o_v + F_WIDTH
    for l in range(DEPTH):
        x = x + 0.5 * _swiglu(_rms(x, g_ffn1[l]), w_up1[l], w_down1[l])
        h = _rms(x, g_mix[l])
        z = h @ w_in[l]
        q, k, v = z[..., :o_q], z[..., o_q:o_k], z[..., o_k:o_v]
        f = z[..., o_v:o_f]
        gates = jax.nn.sigmoid(z[..., o_f:] + b_gate[l])
        gate_a, gate_b = gates[..., :D_MODEL], gates[..., D_MODEL:]
        y_a = _window_attention(q, k, v, sink[l], rel_bias) @ w_branch_a[l]
        y_b = _fourier_mix(f) @ w_branch_b[l]
        x = x + (gate_a * y_a + gate_b * y_b) @ w_out[l]
        x = x + 0.5 * _swiglu(_rms(x, g_ffn2[l]), w_up2[l], w_down2[l])
    return _rms(x, g_final)


_drawn_inputs = setup_inputs


def setup_inputs(seed=0):
    import zlib

    import numpy as np

    out = dict(_drawn_inputs(seed))
    spreads = {}
    factors = {'g_ffn1': 6.11,
     'g_mix': 7.208,
     'b_gate': 64.0,
     'sink': 8.0,
     'g_ffn2': 7.717,
     'g_final': 8.168}
    for name, (base, spread) in spreads.items():
        noise = np.random.default_rng([zlib.crc32(name.encode()), seed]).standard_normal(out[name].shape)
        drawn = base * np.exp(spread * noise) if base else spread * noise
        out[name] = __import__('jax').numpy.asarray(drawn.astype(out[name].dtype))
    for name, factor in factors.items():
        out[name] = (out[name] * factor).astype(out[name].dtype)
    return out
```

```python
from contextlib import ExitStack

import numpy as np

import concourse.bass as bass
from concourse import mybir

F32 = mybir.dt.float32
F32R = mybir.dt.float32r
ACT = mybir.ActivationFunctionType
ALU = mybir.AluOpType

P = 128
SEQ, D_MODEL, D_FF = 512, 1024, 2816
N_HEADS, N_KV, HD = 8, 2, 64
GQ = N_HEADS // N_KV
BLK = WINDOW = 128
N_BUCKETS, MAX_DIST = 32, 128
N_FGROUPS, FG_DIM = 4, 128
Q_WIDTH, KV_WIDTH, F_WIDTH = N_HEADS * HD, N_KV * HD, N_FGROUPS * FG_DIM
EPS, NEG = 1e-6, -1e30

DK = D_MODEL // P
FK = D_FF // P
TB = SEQ // P
SLOTS = 4
BANKS = 4
DOWN_PARTS = [6, 6, 5, 5]
DOWN_AT = [sum(DOWN_PARTS[:i]) for i in range(len(DOWN_PARTS))]
assert sum(DOWN_PARTS) == FK and len(DOWN_PARTS) == SLOTS

G_UP = [0, None]
G_DOWN = [2 * FK, None]
G_K = G_DOWN[0] + SLOTS * DK
G_V, G_Q, G_F = G_K + 1, G_K + 2, G_K + 2 + GQ
G_MIX = G_F + N_FGROUPS
G_OUT = G_MIX + 4 * DK
G_UP[1] = G_OUT + DK
G_DOWN[1] = G_UP[1] + 2 * FK
G_END = G_DOWN[1] + SLOTS * DK
O_UP = [0, None]
O_DOWN = [2 * FK, None]
O_K = O_DOWN[0] + DK
O_V, O_Q, O_F = O_K + 1, O_K + 2, O_K + 2 + GQ
O_MIX = O_F + N_FGROUPS
O_OUT = O_MIX + 4 * DK
O_UP[1] = O_OUT + DK
O_DOWN[1] = O_UP[1] + 2 * FK
NORM_FFN1, NORM_MIX, NORM_FFN2, NORM_FINAL = range(4)
B_PT, B_O, B_S, B_FT = 2, 3, 4, 6
B_SUM, B_RSTD = 4, 5
NPOS = SEQ // 2 + 2
CH_AT = TB * 2 * NPOS
TABLE = CH_AT + 2 * FG_DIM
NREL = 2 * WINDOW + 1
ROWS = 4 * DK + 2 * DK


def t5_buckets():
    rel = np.arange(-WINDOW, WINDOW + 1)
    half = N_BUCKETS // 2
    max_exact = half // 2
    n = np.abs(rel)
    n_safe = np.maximum(n, 1).astype(np.float32)
    large = max_exact + (np.log(n_safe / max_exact) / np.log(MAX_DIST / max_exact)
                         * (half - max_exact)).astype(np.int32)
    large = np.minimum(large, half - 1)
    return (rel > 0).astype(np.int32) * half + np.where(n < max_exact, n, large)


def shape_constants():
    s, k = np.arange(SEQ)[:, None], np.arange(NPOS)[None, :]
    turn = 2 * np.pi * ((s * k) % SEQ) / SEQ
    scale = 1.0 / np.sqrt(SEQ * FG_DIM)
    pos = np.concatenate([np.cos(turn) * scale, -np.sin(turn) * scale], axis=1)
    pos = pos.reshape(TB, P, 2 * NPOS).transpose(1, 0, 2).reshape(P, CH_AT)
    c = np.arange(FG_DIM)
    turn = 2 * np.pi * ((c[:, None] * c[None, :]) % FG_DIM) / FG_DIM
    tables = np.concatenate([pos, np.cos(turn), np.sin(turn)], axis=1).astype(np.float32)
    onehot = np.zeros((N_BUCKETS, NREL + 1), np.float32)
    onehot[t5_buckets(), np.arange(NREL)] = 1.0
    return {"tables": tables, "onehot": onehot}


def window(nb):
    blocks = [j for j in (nb - 1, nb, nb + 1) if 0 <= j < TB]
    return blocks, blocks[0] - (nb - 1)


def mixer_schedule():
    steps = []
    piece = 0
    pieces = 7 * N_FGROUPS
    units = TB * N_KV
    steps.append(("scores", 0))
    for _ in range(4):
        steps.append(("fourier", piece))
        piece += 1
    steps.append(("normalize", 0))
    for u in range(units):
        if u + 1 < units:
            steps.append(("scores", u + 1))
        for b in range(len(window(u // N_KV)[0])):
            steps.append(("turn", u, b))
            if piece < pieces:
                steps.append(("fourier", piece))
                piece += 1
            steps.append(("values", u, b))
        if u + 1 < units:
            steps.append(("normalize", u + 1))
    while piece < pieces:
        steps.append(("fourier", piece))
        piece += 1
    return steps


def granule_tiles(g):
    for down in G_DOWN:
        if down <= g < down + SLOTS * DK:
            return DOWN_PARTS[(g - down) % SLOTS]
    if G_MIX <= g < G_OUT and (g - G_MIX) % 4 >= 2:
        return GQ
    return DK


def turn_index(u, b):
    return sum(len(window(v // N_KV)[0]) for v in range(u)) + b


def build(nc, io):
    x, out = io["x"], io["out"]
    w_up = [io["w_up1"][0].rearrange("(k p) n -> p k n", p=P), io["w_up2"][0].rearrange("(k p) n -> p k n", p=P)]
    w_down = [io["w_down1"][0].rearrange("(k p) n -> p k n", p=P), io["w_down2"][0].rearrange("(k p) n -> p k n", p=P)]
    w_in = io["w_in"][0].rearrange("(k p) n -> p k n", p=P)
    w_a = io["w_branch_a"][0]
    w_b = io["w_branch_b"][0].rearrange("(k p) n -> p k n", p=P)
    w_out = io["w_out"][0].rearrange("(k p) n -> p k n", p=P)
    bias_rows = nc.dram_tensor("bias_rows", [N_HEADS, P, SEQ], F32, kind="Internal").ap()
    steps = mixer_schedule()

    with ExitStack() as ctx:
        base = 16512
        at = [base]

        def place(name, shape, dt, offset=None):
            here = at[0] if offset is None else offset
            size = int(np.prod(shape[1:])) * 4
            t = nc.alloc_sbuf_tensor_at(name, shape, dt, offset=here)
            if offset is None:
                at[0] = here + (size + 31) // 32 * 32
            return t, here, (size + 31) // 32 * 32

        xT, _, _ = place("xT", [P, DK * SEQ], F32)
        h_hi, h_at, _ = place("h_hi", [P, DK * SEQ], F32R)
        h_lo, _, _ = place("h_lo", [P, DK * SEQ], F32R)
        raw, _, _ = place("raw", [P, SLOTS, DK, P], F32)
        w_hi, _, _ = place("w_hi", [P, SLOTS, DK, P], F32R)
        w_lo, _, _ = place("w_lo", [P, SLOTS, DK, P], F32R)
        rstd, _, _ = place("rstd", [P, SEQ], F32)
        ident, _, _ = place("ident", [P, P], F32)
        ones, _, _ = place("ones", [P, P], F32)
        ssum, ssum_at, _ = place("ssum", [P, SEQ], F32)
        sq, _, _ = place("sq", [P, 2, SEQ], F32)
        ga_t, _, _ = place("ga_t", [P, SEQ], F32)
        gb_t, _, _ = place("gb_t", [P, SEQ], F32)
        ua_t, ua_at, _ = place("ua_t", [P, SEQ], F32)
        ub_t, _, _ = place("ub_t", [P, SEQ], F32)
        at[0] += SEQ * 4
        gate_t, up_t = [ga_t, gb_t], [ua_t, ub_t]
        s_a, _, _ = place("s_a", [P, GQ, 3 * BLK], F32, ssum_at)
        s_b, _, _ = place("s_b", [P, GQ, 3 * BLK], F32, ua_at)
        s_t = [s_a, s_b]
        even_t, _, _ = place("even_t", [P, NPOS], F32)
        y_t, _, _ = place("y_t", [P, SEQ], F32)
        consts, _, _ = place("consts", [P, ROWS], F32)
        rows = y_t
        sink, _, _ = place("sink", [P, N_HEADS], F32)
        half, _, _ = place("half", [P, TB], F32)
        var, _, _ = place("var", [P, TB], F32)
        rinv, _, _ = place("rinv", [P, TB], F32)
        mx, _, _ = place("mx", [P, 2, GQ], F32)
        negm, _, _ = place("negm", [P, 2, GQ], F32)
        sdiff, _, _ = place("sdiff", [P, 2, GQ], F32)
        psumr, _, _ = place("psumr", [P, 2, GQ], F32)
        esink, _, _ = place("esink", [P, 2, GQ], F32)
        den, _, _ = place("den", [P, 2, GQ], F32)
        rden, _, _ = place("rden", [P, 2, GQ], F32)
        a_hi, act_at, a_size = place("a_hi", [P, FK * SEQ], F32R)
        a_lo, _, _ = place("a_lo", [P, FK * SEQ], F32R)
        assert at[0] <= nc.sbuf_usable_end, (at[0], nc.sbuf_usable_end)
        act_end = at[0]
        x_rows, _, xr_size = place("x_rows", [P, TB, D_MODEL], F32, act_at)
        bias_wide, bw_at, bw_size = place("bias_wide", [P, N_HEADS, SEQ], F32, act_at + xr_size)
        bias_lhs, bl_at, bl_size = place("bias_lhs", [N_BUCKETS, N_HEADS, P], F32, bw_at + bw_size)
        table_b, _, _ = place("table_b", [N_BUCKETS, N_HEADS], F32, bl_at + bl_size)
        onehot, _, _ = place("onehot", [N_BUCKETS, NREL + 1], F32, bl_at + bl_size + 32)
        here = [act_at]

        def reuse(name, shape, dt):
            t, _, size = place(name, shape, dt, here[0])
            here[0] += size
            assert here[0] <= act_end
            return t

        kp_hi = reuse("kp_hi", [P, N_KV, SEQ], F32R)
        kp_lo = reuse("kp_lo", [P, N_KV, SEQ], F32R)
        v_hi = reuse("v_hi", [P, TB, P], F32R)
        v_lo = reuse("v_lo", [P, TB, P], F32R)
        bias = reuse("bias", [P, N_HEADS, 3 * BLK], F32)
        tab_hi = reuse("tab_hi", [P, TABLE], F32R)
        tab_lo = reuse("tab_lo", [P, TABLE], F32R)
        qo_hi = reuse("qo_hi", [P, GQ, SEQ], F32R)
        qo_lo = reuse("qo_lo", [P, GQ, SEQ], F32R)
        fy_hi = reuse("fy_hi", [P, N_FGROUPS, SEQ], F32R)
        fy_lo = reuse("fy_lo", [P, N_FGROUPS, SEQ], F32R)
        tab_raw, _, _ = place("tab_raw", [P, TABLE], F32, here[0])
        ab_hi = reuse("ab_hi", [P, TB, 2 * FG_DIM], F32R)
        ab_lo = reuse("ab_lo", [P, TB, 2 * FG_DIM], F32R)
        pt_hi = reuse("pt_hi", [P, GQ * BLK], F32R)
        pt_lo = reuse("pt_lo", [P, GQ * BLK], F32R)
        m_hi, _, m_size = place("m_hi", [P, DK * SEQ], F32R, act_at)
        m_lo, _, _ = place("m_lo", [P, DK * SEQ], F32R, act_at + m_size)
        y_rows, _, _ = place("y_rows", [P, TB, D_MODEL], F32, h_at)

        banks = [ctx.enter_context(nc.psum_tensor(f"bank{i}", [P, SEQ], F32)) for i in range(8)]

        def sem(name):
            return ctx.enter_context(nc.semaphore(name))

        x_landed = [sem(f"x_landed{i}") for i in range(4)]
        rows_landed, buckets_landed, sink_landed = sem("rows_landed"), sem("buckets_landed"), sem("sink_landed")
        raw_landed = [sem(f"raw_landed{i}") for i in range(SLOTS)]
        q_second, a_second = [sem(f"q_second{i}") for i in range(GQ)], sem("a_second")
        bias_stored, bias_landed, tables_landed = sem("bias_stored"), sem("bias_landed"), sem("tables_landed")
        out_stored = sem("out_stored")
        ident_ready, fills_ready = sem("ident_ready"), sem("fills_ready")
        sum_added, rinv_ready, zeros_ready = sem("sum_added"), sem("rinv_ready"), sem("zeros_ready")
        w_hi_ready, h_hi_ready, sq_ready = sem("w_hi_ready"), sem("h_hi_ready"), sem("sq_ready")
        silu_ready, a_hi_ready, gate_ready = sem("silu_ready"), sem("a_hi_ready"), sem("gate_ready")
        proj_hi_ready, tab_hi_ready, exp_ready = sem("proj_hi_ready"), sem("tab_hi_ready"), sem("exp_ready")
        pt_hi_ready, o_hi_ready, ab_hi_ready = sem("pt_hi_ready"), sem("o_hi_ready"), sem("ab_hi_ready")
        even_copied, y_hi_ready, m_hi_ready = sem("even_copied"), sem("y_hi_ready"), sem("m_hi_ready")
        y_rows_ready, scaled_act = sem("y_rows_ready"), sem("scaled_act")
        w_lo_ready, h_lo_ready, x_ready = sem("w_lo_ready"), sem("h_lo_ready"), sem("x_ready")
        out_read, product_ready, a_lo_ready = sem("out_read"), sem("product_ready"), sem("a_lo_ready")
        consts_ready, lhs_ready, wide_ready = sem("consts_ready"), sem("lhs_ready"), sem("wide_ready")
        var_ready, diag_ready, rstd_ready = sem("var_ready"), sem("diag_ready"), sem("rstd_ready")
        proj_lo_ready, v_lo_ready, tab_lo_ready = sem("proj_lo_ready"), sem("v_lo_ready"), sem("tab_lo_ready")
        v_hi_ready = sem("v_hi_ready")
        s_read, max_ready, den_ready, probs_ready = sem("s_read"), sem("max_ready"), sem("den_ready"), sem("probs_ready")
        pt_lo_ready, o_lo_ready, ab_lo_ready = sem("pt_lo_ready"), sem("o_lo_ready"), sem("ab_lo_ready")
        y_ready, y_lo_ready = sem("y_ready"), sem("y_lo_ready")
        mixed, m_lo_ready, scaled_dve = sem("mixed"), sem("m_lo_ready"), sem("scaled_dve")
        w_used, turned, consts_turned, bias_done = sem("w_used"), sem("turned"), sem("consts_turned"), sem("bias_done")
        sum_done, rstd_done, v_turned = sem("sum_done"), sem("rstd_done"), sem("v_turned")
        s_done, pt_done, o_done = sem("s_done"), sem("pt_done"), sem("o_done")
        pt_used = sem("pt_used")
        ab_done, even_done, odd_done, y_turned = sem("ab_done"), sem("even_done"), sem("odd_done"), sem("y_turned")

        block = ctx.enter_context(nc.Block())

        def tile(t, m):
            if isinstance(m, int):
                return t[:, m * SEQ:(m + 1) * SEQ]
            return t[:, bass.ds(m * SEQ, SEQ)]

        def gain(n, m):
            if isinstance(m, int):
                return consts[:, n * DK + m:n * DK + m + 1]
            return consts[:, bass.ds(m + n * DK, 1)]


        @block.sync
        def _(sp):
            def load(g, dst, src, it=0, n=0):
                if g >= SLOTS or n:
                    sp.wait_ge(w_lo_ready, g - SLOTS + 1 + n * it)
                sp.dma_start(dst, src).then_inc(raw_landed[g % SLOTS], 16)

            def up(r, it, j, n=0):
                g = G_UP[r] + j
                col = it * (2 * P) + (j // 2) * P + (j % 2) * D_FF
                cols = slice(col, col + P) if isinstance(it, int) else bass.ds(sp.snap(col), P)
                load(g, raw[:, g % SLOTS, :, :], w_up[r][:, :, cols], it, n)

            def down(r, m, j, n=0):
                g = G_DOWN[r] + j
                k0, nk = DOWN_AT[j], DOWN_PARTS[j]
                load(g, raw[:, g % SLOTS, 0:nk, :], w_down[r][:, k0:k0 + nk, bass.ds(sp.snap(m * P), P)], m, n)

            xv = x[0].rearrange("(t p) d -> p t d", p=P)
            for c in range(4):
                w = D_MODEL // 4
                sp.dma_start(x_rows[:, :, c * w:(c + 1) * w], xv[:, :, c * w:(c + 1) * w]).then_inc(x_landed[c], 16)
            for r in range(2):
                if r == 0:
                    for j in range(SLOTS):
                        up(0, 0, j)
                with sp.Fori(1 - r, FK // 2) as it:
                    for j in range(SLOTS):
                        up(r, it, j, SLOTS)
                with sp.Fori(0, DK) as m:
                    for j in range(SLOTS):
                        down(r, m, j, SLOTS)
                if r == 1:
                    break
                for g, col in ((G_K, Q_WIDTH), (G_V, Q_WIDTH + KV_WIDTH)):
                    load(g, raw[:, g % SLOTS, :, :], w_in[:, :, col:col + P])
                for c in range(GQ):
                    g = G_Q + c
                    src = w_in[:, :, 0:Q_WIDTH].rearrange("p k (v c d) -> p k v c d", v=N_KV, c=GQ)[:, :, :, c, :]
                    for v in range(N_KV):
                        if v == 0:
                            load(g, raw[:, g % SLOTS, :, 0:HD], src[:, :, 0, :])
                        else:
                            sp.dma_start(raw[:, g % SLOTS, :, HD:P], src[:, :, 1, :]).then_inc(q_second[c], 16)
                for c in range(N_FGROUPS):
                    g, col = G_F + c, Q_WIDTH + 2 * KV_WIDTH + c * FG_DIM
                    load(g, raw[:, g % SLOTS, :, :], w_in[:, :, col:col + P])
                gates_at = Q_WIDTH + 2 * KV_WIDTH + F_WIDTH
                wa_v = w_a.rearrange("(v c d) n -> v d c n", v=N_KV, c=GQ)
                with sp.Fori(0, DK) as m:
                    for j in range(2):
                        g = G_MIX + j
                        load(g, raw[:, g % SLOTS, :, :], w_in[:, :, bass.ds(sp.snap(m * P + (gates_at + j * D_MODEL)), P)], m, SLOTS)
                    tile_cols = bass.ds(sp.snap(m * P), P)
                    g = G_MIX + 2
                    load(g, raw[HD:P, g % SLOTS, 0:GQ, :], wa_v[1, :, :, tile_cols], m, SLOTS)
                    sp.dma_start(raw[0:HD, g % SLOTS, 0:GQ, :], wa_v[0, :, :, tile_cols]).then_inc(a_second, 16)
                    g = G_MIX + 3
                    load(g, raw[:, g % SLOTS, 0:N_FGROUPS, :], w_b[:, :, tile_cols], m, SLOTS)
                with sp.Fori(0, DK // SLOTS) as it:
                    for j in range(SLOTS):
                        g = G_OUT + j
                        load(g, raw[:, g % SLOTS, :, :], w_out[:, :, bass.ds(sp.snap(it * (SLOTS * P) + j * P), P)], it, SLOTS)
            ov = out[0].rearrange("(t p) d -> p t d", p=P)
            for t in range(TB):
                if t % 2:
                    sp.wait_ge(scaled_act, t // 2 + 1)
                else:
                    sp.wait_ge(scaled_dve, t // 2 + 1)
                sp.dma_start(ov[:, t, :], y_rows[:, t, :]).then_inc(out_stored, 16)
            sp.wait_ge(out_stored, 16 * TB)

        @block.scalar
        def _(act):
            def copy(dst, src, scale=1.0):
                return nc.scalar.activation(dst, src, ACT.Copy, scale=scale)

            def split_hi(g, it=0, n=0):
                s, static = g % SLOTS, isinstance(it, int)
                nk = granule_tiles(g + n * it if static else g)
                act.wait_ge(raw_landed[s], 16 * (g // SLOTS + 1) + 4 * n * it)
                if static and G_Q <= g + n * it < G_Q + GQ:
                    act.wait_ge(q_second[g + n * it - G_Q], 16)
                if static and g + n * it == G_MIX + 2:
                    act.wait_ge(a_second, 16)
                if not static and g == G_MIX + 6:
                    act.wait_ge(a_second, 16 * it + 32)
                if g >= SLOTS:
                    act.wait_ge(w_used, g - SLOTS + 1 + n * it)
                copy(w_hi[:, s, 0:nk, :], raw[:, s, 0:nk, :]).then_inc(w_hi_ready, 1)

            def square_free(n, m):
                if not isinstance(m, int) or m >= 3:
                    act.wait_ge(sum_added, m + ((DK - 1) * n - 2))

            def residual(n, m, odd, first=False):
                if n < NORM_FINAL:
                    copy(tile(h_hi, m), tile(xT, m), scale=gain(n, m)).then_inc(h_hi_ready, 1)
                else:
                    copy(gate_t[odd][:, :], tile(xT, m), scale=gain(n, m)).then_inc(h_hi_ready, 1)
                dst = ssum[:, :] if first else sq[:, odd, :]
                nc.scalar.activation(dst, tile(xT, m), ACT.Square).then_inc(sq_ready, 1)

            r0 = 0
            for name, nr in (("g_ffn1", DK), ("g_mix", DK), ("g_ffn2", DK), ("g_final", DK), ("b_gate", 2 * DK)):
                v = io[name] if name == "g_final" else io[name][0]
                act.dma_start(rows[r0:r0 + nr, 0:P], v.rearrange("(r p) -> r p", p=P)).then_inc(rows_landed, 16)
                r0 += nr
            act.dma_start(table_b[:, :], io["rel_bias"]).then_inc(buckets_landed, 16)
            act.dma_start(onehot[:, :], io["onehot"]).then_inc(buckets_landed, 16)
            act.dma_start(sink[:, :], io["sink"].broadcast_to([P, N_HEADS])).then_inc(sink_landed, 16)

            act.wait_ge(consts_ready, 1)
            for m in range(DK):
                square_free(NORM_FFN1, m)
                act.wait_ge(x_ready, m + 1)
                residual(NORM_FFN1, m, m % 2, m == 0)
                if m % 2:
                    split_hi(m // 2)
            act.wait_ge(wide_ready, N_HEADS)
            act.dma_start(bias_rows.rearrange("h q m -> q h m"), bias_wide[:, :, :]).then_inc(bias_stored, 16)
            act.wait_ge(bias_stored, 16)

            def ffn_up(r, it, n=SLOTS):
                for j in range(2):
                    g, o = G_UP[r] + 2 * j, O_UP[r] + 2 * j
                    split_hi(g + SLOTS, it, n)
                    act.wait_ge(out_read, o + 1 + n * it)
                    nc.scalar.activation(gate_t[j][:, :], gate_t[j][:, :], ACT.Silu).then_inc(silu_ready, 1)
                    split_hi(g + 1 + SLOTS, it, n)
                    act.wait_ge(product_ready, FK * r + j + 1 + 2 * it)
                    copy(tile(a_hi, 2 * it + j), up_t[j][:, :]).then_inc(a_hi_ready, 1)

            def turned_rows(m, odd):
                act.wait_ge(y_turned, m + 1)
                dst = y_rows[:, :, m * P:(m + 1) * P] if isinstance(m, int) else y_rows[:, :, bass.ds(m * P, P)]
                copy(dst, banks[6 + odd][:, :].rearrange("p (t d) -> p t d", t=TB)).then_inc(y_rows_ready, 1)

            def ffn_down(r, it, first=False, last=False, n=2 * SLOTS):
                for j in range(2):
                    g, m = G_DOWN[r] + SLOTS * j, 2 * it + j
                    ahead = not (r == 1 and last and j == 1)
                    if ahead:
                        for i in range(3):
                            split_hi(g + SLOTS + i, it, n)
                    if r == 1 and not (first and j == 0):
                        turned_rows(m - 1, 1 - j)
                    nrm = NORM_MIX if r == 0 else NORM_FINAL
                    square_free(nrm, m)
                    act.wait_ge(out_read, O_DOWN[r] + j + 1 + 2 * it)
                    residual(nrm, m, j, first and j == 0)
                    if ahead:
                        split_hi(g + SLOTS + 3, it, n)

            for r in range(2):
                with act.Fori(0, FK // 2 - 1) as it:
                    ffn_up(r, it)
                ffn_up(r, FK // 2 - 1)
                ffn_down(r, 0, first=True)
                with act.Fori(1, DK // 2 - 1) as it:
                    ffn_down(r, it)
                ffn_down(r, DK // 2 - 1, last=True)
                if r == 1:
                    break

                act.dma_start(tab_raw[:, :], io["tables"]).then_inc(tables_landed, 16)
                diagonals = bias_rows.rearrange("h q m -> h (q m)")[:, BLK - 1:BLK - 1 + P * (SEQ - 1)]
                diagonals = diagonals.rearrange("h (q m) -> q h m", m=SEQ - 1)[:, :, 0:3 * BLK]
                act.dma_start(bias[:, :, :], diagonals).then_inc(bias_landed, 16)
                split_hi(G_K + SLOTS)
                act.wait_ge(zeros_ready, 2)
                act.wait_ge(out_read, O_K + 1)
                for v in range(N_KV):
                    rows_v = slice(v * HD, (v + 1) * HD)
                    last = copy(kp_hi[rows_v, v, :], ga_t[rows_v, :])
                last.then_inc(proj_hi_ready, 1)
                split_hi(G_V + SLOTS)
                act.wait_ge(tables_landed, 16)
                copy(tab_hi[:, :], tab_raw[:, :]).then_inc(tab_hi_ready, 1)
                for c in range(GQ):
                    split_hi(G_Q + c + SLOTS)
                    if c == 1:
                        act.wait_ge(v_turned, 1)
                        copy(v_hi[:, :, :], banks[B_FT][:, :]).then_inc(v_hi_ready, 1)
                    act.wait_ge(out_read, O_Q + c + 1)
                    copy(qo_hi[:, c, :], gate_t[c % 2][:, :]).then_inc(proj_hi_ready, 1)

                for step in steps:
                    if step[0] == "scores":
                        u = step[1]
                        nb, kv = u // N_KV, u % N_KV
                        width = len(window(nb)[0]) * BLK
                        act.wait_ge(max_ready, 3 * u + 3)
                        for c in range(GQ):
                            sc = s_t[u % 2][:, c, 0:width]
                            nc.scalar.activation(sc, sc, ACT.Exp, bias=negm[:, u % 2, c:c + 1],
                                                 accum_out=psumr[:, u % 2, c:c + 1])
                        nc.scalar.activation(esink[:, u % 2, :], sdiff[:, u % 2, :], ACT.Exp).then_inc(exp_ready, 1)
                    elif step[0] == "turn":
                        t = turn_index(*step[1:])
                        act.wait_ge(pt_done, t + 1)
                        if t:
                            act.wait_ge(pt_used, t)
                        copy(pt_hi[:, :], banks[B_PT][:, :]).then_inc(pt_hi_ready, 1)
                    elif step[0] == "values":
                        u, b = step[1:]
                        nb, kv = u // N_KV, u % N_KV
                        if b == len(window(nb)[0]) - 1:
                            rows_v = slice(kv * HD, (kv + 1) * HD)
                            act.wait_ge(pt_used, turn_index(u, b) + 1)
                            copy(qo_hi[rows_v, :, nb * BLK:(nb + 1) * BLK],
                                 banks[B_O][rows_v, :].rearrange("p (c q) -> p c q", c=GQ)).then_inc(o_hi_ready, 1)
                    elif step[0] == "fourier":
                        grp, part = step[1] // 7, step[1] % 7
                        if part == 3:
                            split_hi(G_F + grp + SLOTS)
                            act.wait_ge(out_read, O_F + grp + 1)
                            copy(fy_hi[:, grp, :], gate_t[grp % 2][:, :]).then_inc(proj_hi_ready, 1)
                        elif part == 4:
                            for i in range(2):
                                act.wait_ge(ab_done, 2 * grp + i + 1)
                                if grp and i == 0:
                                    act.wait_ge(odd_done, grp)
                                copy(ab_hi[:, 2 * i:2 * i + 2, :], banks[B_FT + i][:, :]).then_inc(ab_hi_ready, 1)
                        elif part == 5:
                            act.wait_ge(even_done, grp + 1)
                            if grp:
                                act.wait_ge(y_ready, 2 * grp)
                            copy(even_t[:, :], banks[B_FT][:, 0:NPOS]).then_inc(even_copied, 1)
                        elif part == 6:
                            act.wait_ge(y_ready, 2 * grp + 2)
                            copy(fy_hi[:, grp, :], y_t[:, :]).then_inc(y_hi_ready, 1)

                def mix(m, n=SLOTS):
                    for i in range(2):
                        split_hi(G_MIX + i + SLOTS, m, n)
                        act.wait_ge(out_read, O_MIX + i + 1 + n * m)
                        b = 4 * DK + i * DK
                        b_gate = consts[:, b + m:b + m + 1] if isinstance(m, int) else consts[:, bass.ds(m + b, 1)]
                        nc.scalar.activation(gate_t[i][:, :], gate_t[i][:, :], ACT.Sigmoid,
                                             bias=b_gate).then_inc(gate_ready, 1)
                    split_hi(G_MIX + 2 + SLOTS, m, n)
                    split_hi(G_MIX + 3 + SLOTS, m, n)
                    act.wait_ge(mixed, m + 1)
                    copy(tile(m_hi, m), ua_t[:, :]).then_inc(m_hi_ready, 1)

                with act.Fori(0, DK - 1) as m:
                    mix(m)
                mix(DK - 1)
                for m in range(DK):
                    split_hi(G_OUT + m + SLOTS)
                    square_free(NORM_FFN2, m)
                    act.wait_ge(out_read, O_OUT + m + 1)
                    residual(NORM_FFN2, m, m % 2, m == 0)

            turned_rows(DK - 1, 1)
            act.wait_ge(rinv_ready, NORM_FINAL + 1)
            act.wait_ge(y_rows_ready, DK)
            for t in range(1, TB, 2):
                copy(y_rows[:, t, :], y_rows[:, t, :], scale=rinv[:, t:t + 1]).then_inc(scaled_act, 1)

        @block.vector
        def _(dve):
            vec = nc.vector

            def split_lo(g, it=0, n=0):
                s = g % SLOTS
                nk = granule_tiles(g + n * it if isinstance(it, int) else g)
                dve.wait_ge(w_hi_ready, g + 1 + n * it)
                vec.tensor_tensor(w_lo[:, s, 0:nk, :], raw[:, s, 0:nk, :], w_hi[:, s, 0:nk, :].bitcast(F32),
                                  ALU.subtract).then_inc(w_lo_ready, 1)

            def lo(dst, full, hi):
                return vec.tensor_tensor(dst, full, hi.bitcast(F32), ALU.subtract)

            def new_h_lo(n, m):
                dve.wait_ge(h_hi_ready, m + (DK * n + 1))
                vec.scalar_tensor_tensor(out=tile(h_lo, m), in0=tile(xT, m), scalar=gain(n, m),
                                         in1=tile(h_hi, m).bitcast(F32), op0=ALU.mult,
                                         op1=ALU.subtract).then_inc(h_lo_ready, 1)

            def norm_factors(n):
                mean(n)
                dve.wait_ge(rinv_ready, n + 1)
                for t in range(TB):
                    last = vec.tensor_scalar(gb_t[:, t * P:(t + 1) * P], ident[:, :], rinv[:, t:t + 1], None, ALU.mult)
                last.then_inc(diag_ready, 1)
                dve.wait_ge(rstd_done, n + 1)
                vec.tensor_copy(rstd[:, :], banks[B_RSTD][:, :]).then_inc(rstd_ready, 1)
                dve.wait_ge(rstd_ready, n + 1)

            def mean(n):
                dve.wait_ge(sum_done, n + 1)
                vec.tensor_scalar(var[:, :], banks[B_SUM][:, 0:2 * TB:2], 1.0 / D_MODEL, EPS, ALU.mult,
                                  ALU.add).then_inc(var_ready, 1)

            dve.wait_ge(buckets_landed, 32)
            vec.tensor_copy(bias_lhs[:, :, :], table_b[:, :].unsqueeze(2).broadcast_to([N_BUCKETS, N_HEADS, P])
                            ).then_inc(lhs_ready, 1)
            dve.wait_ge(consts_turned, 1)
            vec.tensor_copy(consts[:, :], banks[7][:, 0:ROWS]).then_inc(consts_ready, 1)
            dve.wait_ge(fills_ready, 3)
            for h in range(N_HEADS):
                dve.wait_ge(bias_done, h + 1)
                vec.tensor_copy(bias_wide[:, h, P - 1:P - 1 + NREL], banks[h % 4][:, 0:NREL]).then_inc(wide_ready, 1)
            dve.wait_ge(consts_ready, 1)
            for m in range(DK):
                dve.wait_ge(turned, m + 1)
                vec.tensor_copy(tile(xT, m), banks[4 + m % 4][:, :]).then_inc(x_ready, 1)
                if m % 2 == 0 and m:
                    split_lo(m // 2 - 1)
                dve.wait_ge(x_ready, m + 1)
                new_h_lo(NORM_FFN1, m)
            split_lo(SLOTS - 1)

            def ffn_up(r, it, first=False, n=SLOTS):
                for j in range(2):
                    g, o, f = G_UP[r] + 2 * j, O_UP[r] + 2 * j, FK * r + j
                    split_lo(g + SLOTS, it, n)
                    if first and j == 0:
                        norm_factors(NORM_FFN1 if r == 0 else NORM_FFN2)
                    dve.wait_ge(w_used, g + 1 + n * it)
                    vec.tensor_tensor(gate_t[j][:, :], banks[o % BANKS][:, :], rstd[:, :], ALU.mult).then_inc(out_read, 1)
                    split_lo(g + 1 + SLOTS, it, n)
                    dve.wait_ge(w_used, g + 2 + n * it)
                    vec.tensor_tensor(up_t[j][:, :], banks[(o + 1) % BANKS][:, :], rstd[:, :], ALU.mult).then_inc(out_read, 1)
                    dve.wait_ge(out_read, o + 2 + n * it)
                    dve.wait_ge(silu_ready, f + 1 + 2 * it)
                    vec.tensor_tensor(up_t[j][:, :], gate_t[j][:, :], up_t[j][:, :], ALU.mult).then_inc(product_ready, 1)
                    dve.wait_ge(a_hi_ready, f + 1 + 2 * it)
                    lo(tile(a_lo, 2 * it + j), up_t[j][:, :], tile(a_hi, 2 * it + j)).then_inc(a_lo_ready, 1)

            def residual(n, m, o, scale, it=0, per=0):
                vec.scalar_tensor_tensor(out=tile(xT, m), in0=banks[o % BANKS][:, :], scalar=scale, in1=tile(xT, m),
                                         op0=ALU.mult, op1=ALU.add).then_inc(out_read, 1)

            def ffn_down(r, it, last=False, n=2 * SLOTS):
                nrm = NORM_MIX if r == 0 else NORM_FINAL
                for j in range(2):
                    g, o, m = G_DOWN[r] + SLOTS * j, O_DOWN[r] + j, 2 * it + j
                    ahead = not (r == 1 and last and j == 1)
                    if ahead:
                        for i in range(3):
                            split_lo(g + SLOTS + i, it, n)
                    dve.wait_ge(w_used, g + SLOTS + n * it)
                    residual(nrm, m, o, 0.5)
                    if ahead:
                        split_lo(g + SLOTS + 3, it, n)
                    if nrm < NORM_FINAL:
                        dve.wait_ge(out_read, o + 1 + 2 * it)
                        new_h_lo(nrm, m)

            for r in range(2):
                ffn_up(r, 0, first=True)
                with dve.Fori(1, FK // 2 - 1) as it:
                    ffn_up(r, it)
                ffn_up(r, FK // 2 - 1)
                with dve.Fori(0, DK // 2 - 1) as it:
                    ffn_down(r, it)
                ffn_down(r, DK // 2 - 1, last=True)
                if r == 1:
                    break

                split_lo(G_K + SLOTS)
                norm_factors(NORM_MIX)
                dve.wait_ge(w_used, G_K + 1)
                vec.tensor_tensor(ga_t[:, :], banks[O_K % BANKS][:, :], rstd[:, :], ALU.mult).then_inc(out_read, 1)
                split_lo(G_V + SLOTS)
                dve.wait_ge(proj_hi_ready, 1)
                for v in range(N_KV):
                    rows_v = slice(v * HD, (v + 1) * HD)
                    last = lo(kp_lo[rows_v, v, :], ga_t[rows_v, :], kp_hi[rows_v, v, :])
                last.then_inc(proj_lo_ready, 1)
                dve.wait_ge(w_used, G_V + 1)
                vec.tensor_tensor(gb_t[:, :], banks[O_V % BANKS][:, :], rstd[:, :], ALU.mult).then_inc(out_read, 1)
                dve.wait_ge(tab_hi_ready, 1)
                lo(tab_lo[:, :], tab_raw[:, :], tab_hi[:, :]).then_inc(tab_lo_ready, 1)
                for c in range(GQ):
                    split_lo(G_Q + c + SLOTS)
                    if c == 1:
                        dve.wait_ge(v_hi_ready, 1)
                        lo(v_lo[:, :, :], banks[B_FT][:, :].rearrange("p (t d) -> p t d", t=TB),
                           v_hi[:, :, :]).then_inc(v_lo_ready, 1)
                    dve.wait_ge(w_used, G_Q + c + 1)
                    if c == 0:
                        dve.wait_ge(proj_lo_ready, 1)
                    vec.scalar_tensor_tensor(out=gate_t[c % 2][:, :], in0=banks[(O_Q + c) % BANKS][:, :],
                                             scalar=HD ** -0.5, in1=rstd[:, :], op0=ALU.mult,
                                             op1=ALU.mult).then_inc(out_read, 1)
                    dve.wait_ge(proj_hi_ready, c + 2)
                    lo(qo_lo[:, c, :], gate_t[c % 2][:, :], qo_hi[:, c, :]).then_inc(proj_lo_ready, 1)

                dve.wait_ge(bias_landed, 16)
                dve.wait_ge(sink_landed, 16)
                for step in steps:
                    if step[0] == "scores":
                        u = step[1]
                        nb, kv, b = u // N_KV, u % N_KV, u % 2
                        blocks, w0 = window(nb)
                        width = len(blocks) * BLK
                        for c in range(GQ):
                            dve.wait_ge(s_done, GQ * u + c + 1)
                            vec.tensor_tensor_reduce(
                                out=s_t[b][:, c, 0:width], in0=banks[B_S + c % 2][:, 0:width],
                                in1=bias[:, GQ * kv + c, w0 * BLK:w0 * BLK + width], scale=1.0, scalar=NEG,
                                op0=ALU.add, op1=ALU.max, accum_out=mx[:, b, c:c + 1]).then_inc(s_read, 1)
                        dve.wait_ge(s_read, GQ * (u + 1))
                        sk = sink[:, GQ * kv:GQ * (kv + 1)]
                        vec.tensor_tensor(mx[:, b, :], mx[:, b, :], sk, ALU.max).then_inc(max_ready, 1)
                        dve.wait_ge(max_ready, 3 * u + 1)
                        vec.tensor_scalar(negm[:, b, :], mx[:, b, :], -1.0, None, ALU.mult).then_inc(max_ready, 1)
                        vec.tensor_tensor(sdiff[:, b, :], sk, mx[:, b, :], ALU.subtract).then_inc(max_ready, 1)
                    elif step[0] == "normalize":
                        u = step[1]
                        b = u % 2
                        width = len(window(u // N_KV)[0]) * BLK
                        dve.wait_ge(exp_ready, u + 1)
                        vec.tensor_tensor(den[:, b, :], psumr[:, b, :], esink[:, b, :], ALU.add).then_inc(den_ready, 1)
                        dve.wait_ge(den_ready, 2 * u + 1)
                        vec.reciprocal(rden[:, b, :], den[:, b, :]).then_inc(den_ready, 1)
                        dve.wait_ge(den_ready, 2 * u + 2)
                        for c in range(GQ):
                            sc = s_t[b][:, c, 0:width]
                            last = vec.tensor_scalar(sc, sc, rden[:, b, c:c + 1], None, ALU.mult)
                        last.then_inc(probs_ready, 1)
                    elif step[0] == "turn":
                        t = turn_index(*step[1:])
                        dve.wait_ge(pt_hi_ready, t + 1)
                        lo(pt_lo[:, :], banks[B_PT][:, :], pt_hi[:, :]).then_inc(pt_lo_ready, 1)
                    elif step[0] == "values":
                        u, b = step[1:]
                        nb, kv = u // N_KV, u % N_KV
                        if b == len(window(nb)[0]) - 1:
                            rows_v, cols = slice(kv * HD, (kv + 1) * HD), slice(nb * BLK, (nb + 1) * BLK)
                            dve.wait_ge(o_hi_ready, u + 1)
                            lo(qo_lo[rows_v, :, cols], banks[B_O][rows_v, :].rearrange("p (c q) -> p c q", c=GQ),
                               qo_hi[rows_v, :, cols]).then_inc(o_lo_ready, 1)
                    elif step[0] == "fourier":
                        grp, part = step[1] // 7, step[1] % 7
                        if part == 3:
                            split_lo(G_F + grp + SLOTS)
                            dve.wait_ge(w_used, G_F + grp + 1)
                            if grp < 2:
                                dve.wait_ge(proj_lo_ready, GQ + grp)
                            vec.tensor_tensor(gate_t[grp % 2][:, :], banks[grp % 2][:, :], rstd[:, :],
                                              ALU.mult).then_inc(out_read, 1)
                            dve.wait_ge(proj_hi_ready, GQ + 2 + grp)
                            lo(fy_lo[:, grp, :], gate_t[grp % 2][:, :], fy_hi[:, grp, :]).then_inc(proj_lo_ready, 1)
                        elif part == 4:
                            for i in range(2):
                                dve.wait_ge(ab_hi_ready, 2 * grp + i + 1)
                                lo(ab_lo[:, 2 * i:2 * i + 2, :],
                                   banks[B_FT + i][:, :].rearrange("p (t d) -> p t d", t=2),
                                   ab_hi[:, 2 * i:2 * i + 2, :]).then_inc(ab_lo_ready, 1)
                        elif part == 6:
                            dve.wait_ge(odd_done, grp + 1)
                            dve.wait_ge(even_copied, grp + 1)
                            h = SEQ // 2
                            vec.tensor_tensor(y_t[:, 0:h + 1], even_t[:, 0:h + 1], banks[B_FT + 1][:, 0:h + 1],
                                              ALU.add).then_inc(y_ready, 1)
                            vec.tensor_tensor(y_t[:, SEQ - 1:h:-1], even_t[:, 1:h], banks[B_FT + 1][:, 1:h],
                                              ALU.subtract).then_inc(y_ready, 1)
                            dve.wait_ge(y_hi_ready, grp + 1)
                            lo(fy_lo[:, grp, :], y_t[:, :], fy_hi[:, grp, :]).then_inc(y_lo_ready, 1)

                def mix(m, n=SLOTS):
                    for i in range(2):
                        split_lo(G_MIX + i + SLOTS, m, n)
                        dve.wait_ge(w_used, G_MIX + i + 1 + n * m)
                        vec.tensor_tensor(gate_t[i][:, :], banks[(O_MIX + i) % BANKS][:, :], rstd[:, :],
                                          ALU.mult).then_inc(out_read, 1)
                    for i in range(2):
                        split_lo(G_MIX + 2 + i + SLOTS, m, n)
                        dve.wait_ge(gate_ready, 2 * m + i + 1)
                        dve.wait_ge(w_used, G_MIX + 3 + i + n * m)
                        vec.tensor_tensor(up_t[i][:, :], banks[(O_MIX + 2 + i) % BANKS][:, :], gate_t[i][:, :],
                                          ALU.mult).then_inc(out_read, 1)
                    dve.wait_ge(out_read, O_MIX + 4 + n * m)
                    vec.tensor_tensor(ua_t[:, :], ua_t[:, :], ub_t[:, :], ALU.add).then_inc(mixed, 1)
                    dve.wait_ge(m_hi_ready, m + 1)
                    lo(tile(m_lo, m), ua_t[:, :], tile(m_hi, m)).then_inc(m_lo_ready, 1)

                with dve.Fori(0, DK - 1) as m:
                    mix(m)
                mix(DK - 1)
                for m in range(DK):
                    split_lo(G_OUT + m + SLOTS)
                    dve.wait_ge(w_used, G_OUT + m + 1)
                    residual(NORM_FFN2, m, O_OUT + m, 1.0)
                    dve.wait_ge(out_read, O_OUT + m + 1)
                    new_h_lo(NORM_FFN2, m)

            mean(NORM_FINAL)
            dve.wait_ge(rinv_ready, NORM_FINAL + 1)
            dve.wait_ge(y_rows_ready, DK)
            for t in range(0, TB, 2):
                vec.tensor_scalar(y_rows[:, t, :], y_rows[:, t, :], rinv[:, t:t + 1], None,
                                  ALU.mult).then_inc(scaled_dve, 1)

        @block.gpsimd
        def _(pool):
            nc.gpsimd.memset(ident[:, :], 0.0).then_inc(ident_ready, 1)
            pool.wait_ge(ident_ready, 1)
            nc.gpsimd.affine_select(out=ident[:, :], in_=ident[:, :], compare_op=ALU.not_equal, fill=1.0, base=0,
                                    pattern=[[-1, P]], channel_multiplier=1).then_inc(ident_ready, 1)
            nc.gpsimd.memset(ones[:, :], 1.0).then_inc(fills_ready, 1)
            nc.gpsimd.memset(half[:, :], -0.5).then_inc(fills_ready, 1)
            nc.gpsimd.memset(bias_wide[:, :, :], NEG).then_inc(fills_ready, 1)
            pool.wait_ge(fills_ready, 3)
            for n in range(4):
                for m in range(1, DK):
                    pool.wait_ge(sq_ready, DK * n + m + 1)
                    if m > 1:
                        pool.wait_ge(sum_added, (DK - 1) * n + m - 1)
                    nc.gpsimd.tensor_tensor(ssum[:, :], ssum[:, :], sq[:, m % 2, :], ALU.add).then_inc(sum_added, 1)
                pool.wait_ge(var_ready, n + 1)
                nc.gpsimd.tensor_tensor(rinv[:, :], var[:, :], half[:, :], ALU.pow).then_inc(rinv_ready, 1)
                if n == NORM_MIX:
                    pool.wait_ge(rinv_ready, n + 1)
                    nc.gpsimd.memset(kp_hi[:, :, :].bitcast(F32), 0.0).then_inc(zeros_ready, 1)
                    nc.gpsimd.memset(kp_lo[:, :, :].bitcast(F32), 0.0).then_inc(zeros_ready, 1)

        @block.tensor
        def _(pe):
            def passes(out_ap, pairs, lo_ready=None, first=True, last=True):
                for i, (w, x_) in enumerate(pairs):
                    nc.tensor.matmul(out_ap, w[0], x_[0], start=first and i == 0, stop=False)
                    nc.tensor.matmul(out_ap, w[0], x_[1], start=False, stop=False)
                if lo_ready is not None:
                    pe.wait_ge(*lo_ready)
                for i, (w, x_) in enumerate(pairs):
                    mm = nc.tensor.matmul(out_ap, w[1], x_[0], start=False, stop=last and i == len(pairs) - 1)
                return mm

            def granule(g, out_ap, x_parts, first=True, last=True, it=0, n=0, tiles=None, x_ready_at=None, done=True):
                s = g % SLOTS
                tiles = tiles if tiles is not None else range(granule_tiles(g))
                pe.wait_ge(w_hi_ready, g + 1 + n * it)
                for i, k in enumerate(tiles):
                    if x_ready_at:
                        x_ready_at(k)
                    xh, xl = x_parts(k)
                    nc.tensor.matmul(out_ap, w_hi[:, s, k, :], xh, start=first and i == 0, stop=False)
                    nc.tensor.matmul(out_ap, w_hi[:, s, k, :], xl, start=False, stop=False)
                pe.wait_ge(w_lo_ready, g + 1 + n * it)
                for i, k in enumerate(tiles):
                    mm = nc.tensor.matmul(out_ap, w_lo[:, s, k, :], x_parts(k)[0], start=False,
                                          stop=last and i == len(tiles) - 1)
                if done:
                    mm.then_inc(w_used, 1)

            def h_parts(k):
                return tile(h_hi, k), tile(h_lo, k)

            def h_ready(n):
                def wait(k):
                    pe.wait_ge(h_hi_ready, DK * n + k + 1)
                    pe.wait_ge(h_lo_ready, DK * n + k + 1)
                return wait

            def sum_squares(n):
                pe.wait_ge(sum_added, (DK - 1) * (n + 1))
                for t in range(TB):
                    mm = nc.tensor.matmul(banks[B_SUM][:, 2 * t:2 * t + 2], ssum[:, t * P:(t + 1) * P], ones[:, 0:2],
                                          start=True, stop=True)
                mm.then_inc(sum_done, 1)

            def spread_factors(n):
                pe.wait_ge(diag_ready, n + 1)
                nc.tensor.matmul(banks[B_RSTD][:, :], ones[:, :], gb_t[:, :], start=True, stop=True).then_inc(rstd_done, 1)

            pe.wait_ge(ident_ready, 2)
            pe.wait_ge(rows_landed, 16 * 5)
            nc.tensor.transpose(banks[7][:, 0:ROWS], rows[0:ROWS, 0:P], ident[0:ROWS, 0:ROWS]).then_inc(consts_turned, 1)
            pe.wait_ge(lhs_ready, 1)
            for h in range(N_HEADS):
                if h >= 4:
                    pe.wait_ge(wide_ready, h - 3)
                nc.tensor.matmul(banks[h % 4][:, 0:NREL + 1], bias_lhs[:, h, :], onehot[:, :], start=True,
                                 stop=True).then_inc(bias_done, 1)
            for m in range(DK):
                if m % 2 == 0:
                    pe.wait_ge(x_landed[m // 2], 16)
                if m >= 4:
                    pe.wait_ge(x_ready, m - 3)
                if m == 3:
                    pe.wait_ge(consts_ready, 1)
                for t in range(TB):
                    mm = nc.tensor.transpose(banks[4 + m % 4][:, t * P:(t + 1) * P],
                                             x_rows[:, t, m * P:(m + 1) * P], ident[:, :])
                mm.then_inc(turned, 1)

            def ffn_up(r, it, first=False, n=SLOTS):
                nrm = NORM_FFN1 if r == 0 else NORM_FFN2
                for j in range(SLOTS):
                    g, o = G_UP[r] + j, O_UP[r] + j
                    if not first or o - 3 > 0:
                        pe.wait_ge(out_read, o - 3 + n * it)
                    granule(g, banks[o % BANKS][:, :], h_parts, it=it, n=n,
                            x_ready_at=h_ready(nrm) if first and j == 0 else None)
                    if first and j == 0:
                        sum_squares(nrm)
                    if first and j == 1:
                        spread_factors(nrm)

            def a_parts(at_):
                return lambda k: (tile(a_hi, at_ + k), tile(a_lo, at_ + k))

            def turn_rows(m, odd):
                pe.wait_ge(h_hi_ready, m + (DK * NORM_FINAL + 1))
                if not isinstance(m, int) or m >= 2:
                    pe.wait_ge(y_rows_ready, m - 1)
                for t in range(TB):
                    mm = nc.tensor.transpose(banks[6 + odd][:, t * P:(t + 1) * P],
                                             gate_t[odd][:, t * P:(t + 1) * P], ident[:, :])
                mm.then_inc(y_turned, 1)

            def ffn_down(r, it, first=False, n=2 * SLOTS):
                for c in range(2):
                    o = O_DOWN[r] + c
                    pe.wait_ge(out_read, o - 1 + 2 * it)
                    for j in range(SLOTS):
                        g = G_DOWN[r] + SLOTS * c + j

                        def a_ready(k, at_=DOWN_AT[j]):
                            if k == 0 or at_ + k >= FK - 2:
                                need = FK * r + (at_ + k + 1 if at_ + k >= FK - 2 else FK - 2)
                                pe.wait_ge(a_hi_ready, need)
                                pe.wait_ge(a_lo_ready, need)

                        granule(g, banks[o % BANKS][:, :], a_parts(DOWN_AT[j]), first=j == 0, last=j == SLOTS - 1,
                                it=it, n=n, x_ready_at=a_ready if c == 0 and j in (0, SLOTS - 1) else None)
                        if r == 1 and j == 1 and not (first and c == 0):
                            turn_rows(2 * it + c - 1, 1 - c)

            for r in range(2):
                ffn_up(r, 0, first=True)
                with pe.Fori(1, FK // 2) as it:
                    ffn_up(r, it)
                ffn_down(r, 0, first=True)
                with pe.Fori(1, DK // 2) as it:
                    ffn_down(r, it)
                if r == 1:
                    break

                pe.wait_ge(out_read, O_K - 1)
                granule(G_K, banks[O_K % BANKS][:, :], h_parts, x_ready_at=h_ready(NORM_MIX))
                sum_squares(NORM_MIX)
                pe.wait_ge(out_read, O_K)
                granule(G_V, banks[O_V % BANKS][:, :], h_parts)
                spread_factors(NORM_MIX)
                for c in range(GQ):
                    pe.wait_ge(out_read, O_Q + c - 3)
                    granule(G_Q + c, banks[(O_Q + c) % BANKS][:, :], h_parts)
                    if c == 0:
                        pe.wait_ge(out_read, O_V + 1)
                        for t in range(TB):
                            mm = nc.tensor.transpose(banks[B_FT][:, t * P:(t + 1) * P], gb_t[:, t * P:(t + 1) * P],
                                                     ident[:, :])
                        mm.then_inc(v_turned, 1)

                for step in steps:
                    if step[0] == "scores":
                        u = step[1]
                        nb, kv = u // N_KV, u % N_KV
                        blocks, _ = window(nb)
                        keys = slice(blocks[0] * BLK, (blocks[-1] + 1) * BLK)
                        width = len(blocks) * BLK
                        for c in range(GQ):
                            if u == 0:
                                pe.wait_ge(proj_lo_ready, c + 2)
                            if GQ * u + c >= 2:
                                pe.wait_ge(s_read, GQ * u + c - 1)
                            q = slice(nb * BLK, (nb + 1) * BLK)
                            passes(banks[B_S + c % 2][:, 0:width],
                                   [((qo_hi[:, c, q], qo_lo[:, c, q]), (kp_hi[:, kv, keys], kp_lo[:, kv, keys]))]
                                   ).then_inc(s_done, 1)
                    elif step[0] == "turn":
                        u, b = step[1:]
                        t = turn_index(u, b)
                        pe.wait_ge(probs_ready, u + 1)
                        if t:
                            pe.wait_ge(pt_lo_ready, t)
                        else:
                            pe.wait_ge(out_read, O_Q + 1)
                        for c in range(GQ):
                            mm = nc.tensor.transpose(banks[B_PT][:, c * BLK:(c + 1) * BLK],
                                                     s_t[u % 2][:, c, b * BLK:(b + 1) * BLK], ident[:, :])
                        mm.then_inc(pt_done, 1)
                    elif step[0] == "values":
                        u, b = step[1:]
                        t = turn_index(u, b)
                        blocks, _ = window(u // N_KV)
                        blk = blocks[b]
                        if t == 0:
                            pe.wait_ge(v_lo_ready, 1)
                            pe.wait_ge(out_read, O_Q + 2)
                        if b == 0 and u:
                            pe.wait_ge(o_lo_ready, u)
                        o_bank = banks[B_O][:, :]
                        pe.wait_ge(pt_hi_ready, t + 1)
                        nc.tensor.matmul(o_bank, v_hi[:, blk, :], pt_hi[:, :], start=b == 0, stop=False)
                        nc.tensor.matmul(o_bank, v_lo[:, blk, :], pt_hi[:, :], start=False, stop=False)
                        pe.wait_ge(pt_lo_ready, t + 1)
                        nc.tensor.matmul(o_bank, v_hi[:, blk, :], pt_lo[:, :], start=False,
                                         stop=b == len(blocks) - 1).then_inc(pt_used, 1)
                    elif step[0] == "fourier":
                        grp, part = step[1] // 7, step[1] % 7
                        if part < 4:
                            if part == 0:
                                pe.wait_ge(out_read, O_F + grp - 1)
                            granule(G_F + grp, banks[grp % 2][:, :], h_parts, first=part == 0, last=part == 3,
                                    tiles=range(2 * part, 2 * part + 2), done=part == 3)
                        elif part == 4:
                            pe.wait_ge(proj_lo_ready, GQ + 2 + grp)
                            if grp == 0:
                                pe.wait_ge(v_lo_ready, 1)
                                pe.wait_ge(tab_lo_ready, 1)
                            else:
                                pe.wait_ge(y_ready, 2 * grp)
                            ch = slice(CH_AT, CH_AT + 2 * FG_DIM)
                            for t in range(TB):
                                tok = slice(t * P, (t + 1) * P)
                                o_ap = banks[B_FT + t // 2][:, (t % 2) * 2 * FG_DIM:(t % 2 + 1) * 2 * FG_DIM]
                                mm = passes(o_ap, [((fy_hi[:, grp, tok], fy_lo[:, grp, tok]),
                                                    (tab_hi[:, ch], tab_lo[:, ch]))])
                                if t % 2:
                                    mm.then_inc(ab_done, 1)
                        else:
                            odd = part - 5
                            pe.wait_ge(ab_lo_ready, 2 * grp + 2)
                            pairs = []
                            for t in range(TB):
                                c0 = slice(odd * FG_DIM, (odd + 1) * FG_DIM)
                                k0 = (2 * t + odd) * NPOS
                                pairs.append(((ab_hi[:, t, c0], ab_lo[:, t, c0]),
                                              (tab_hi[:, k0:k0 + NPOS], tab_lo[:, k0:k0 + NPOS])))
                            passes(banks[B_FT + odd][:, 0:NPOS], pairs).then_inc(odd_done if odd else even_done, 1)

                with pe.Fori(0, DK) as m:
                    pe.wait_ge(pt_lo_ready, turn_index(TB * N_KV, 0))
                    pe.wait_ge(o_lo_ready, TB * N_KV)
                    pe.wait_ge(y_lo_ready, N_FGROUPS)
                    parts = [h_parts, h_parts, lambda k: (qo_hi[:, k, :], qo_lo[:, k, :]),
                             lambda k: (fy_hi[:, k, :], fy_lo[:, k, :])]
                    for j in range(SLOTS):
                        o = O_MIX + j
                        pe.wait_ge(out_read, o - 3 + SLOTS * m)
                        granule(G_MIX + j, banks[o % BANKS][:, :], parts[j], it=m, n=SLOTS)

                def mixed_ready(k):
                    if k == 0 or k == DK - 1:
                        need = DK - 1 if k == 0 else DK
                        pe.wait_ge(m_hi_ready, need)
                        pe.wait_ge(m_lo_ready, need)

                with pe.Fori(0, DK // SLOTS) as it:
                    for j in range(SLOTS):
                        o = O_OUT + j
                        pe.wait_ge(out_read, o - 3 + SLOTS * it)
                        granule(G_OUT + j, banks[o % BANKS][:, :], lambda k: (tile(m_hi, k), tile(m_lo, k)),
                                it=it, n=SLOTS, x_ready_at=mixed_ready if j == 0 else None)

            turn_rows(DK - 1, 1)
            sum_squares(NORM_FINAL)


INPUTS = ["x", "g_ffn1", "w_up1", "w_down1", "g_mix", "w_in", "b_gate", "sink", "rel_bias", "w_branch_a",
          "w_branch_b", "w_out", "g_ffn2", "w_up2", "w_down2", "g_final"]


def kernel(**inputs):
    import concourse.bacc as bacc
    from concourse.bass_utils import run_bass_kernel_spmd

    nc = bacc.Bacc("TRN2", target_bir_lowering=False, num_devices=1)
    arrays, io = {}, {}
    host = {name: np.ascontiguousarray(inputs[name]) for name in INPUTS}
    host.update(shape_constants())
    for name, a in host.items():
        arrays[f"in_{name}_dram"] = a
        io[name] = nc.dram_tensor(f"in_{name}_dram", a.shape, mybir.dt.from_np(a.dtype), kind="ExternalInput").ap()
    io["out"] = nc.dram_tensor("out_dram", (1, SEQ, D_MODEL), F32, kind="ExternalOutput").ap()
    build(nc, io)
    r = run_bass_kernel_spmd(nc, [arrays], core_ids=[0])
    return r.results[0]["out_dram"]
```

```python
from contextlib import ExitStack

import numpy as np

import concourse.bass as bass
from concourse import mybir

F32 = mybir.dt.float32
F32R = mybir.dt.float32r
ACT = mybir.ActivationFunctionType
ALU = mybir.AluOpType

P = 128
SEQ, D_MODEL, D_FF = 512, 1024, 2816
N_HEADS, N_KV, HD = 8, 2, 64
GQ = N_HEADS // N_KV
BLK = WINDOW = 128
N_BUCKETS, MAX_DIST = 32, 128
N_FGROUPS, FG_DIM = 4, 128
Q_WIDTH, KV_WIDTH, F_WIDTH = N_HEADS * HD, N_KV * HD, N_FGROUPS * FG_DIM
EPS, NEG = 1e-6, -1e30

DK = D_MODEL // P
FK = D_FF // P
TB = SEQ // P
SLOTS = 4
BANKS = 4
DOWN_PARTS = [6, 6, 5, 5]
DOWN_AT = [sum(DOWN_PARTS[:i]) for i in range(len(DOWN_PARTS))]
assert sum(DOWN_PARTS) == FK and len(DOWN_PARTS) == SLOTS

G_UP = [0, None]
G_DOWN = [2 * FK, None]
G_F = G_DOWN[0] + SLOTS * DK
G_K = G_F + N_FGROUPS
G_V, G_Q = G_K + 1, G_K + 2
G_B = G_Q + GQ
G_A = G_B + 2 * DK
G_OUT = G_A + 2 * DK
G_UP[1] = G_OUT + DK
G_DOWN[1] = G_UP[1] + 2 * FK
G_END = G_DOWN[1] + SLOTS * DK
O_UP = [0, None]
O_DOWN = [2 * FK, None]
O_F = O_DOWN[0] + DK
O_K = O_F + N_FGROUPS
O_V, O_Q = O_K + 1, O_K + 2
O_B = O_Q + GQ
O_A = O_B + 2 * DK
O_OUT = O_A + 2 * DK
O_UP[1] = O_OUT + DK
O_DOWN[1] = O_UP[1] + 2 * FK
NORM_FFN1, NORM_MIX, NORM_FFN2, NORM_FINAL = range(4)
B_SUM, B_RSTD = 4, 5
B_CH, B_POS = 4, 6
B_S = 4
B_PT, B_O = [2, 6], [3, 7]
NPOS = SEQ // 2 + 2
CH_AT = TB * 2 * NPOS
TABLE = CH_AT + 2 * FG_DIM
X_BANKS = 6
X_ORDER = [("h", 0), ("h", 1), ("w", 0), ("h", 2), ("h", 3), ("x", 0), ("h", 4), ("h", 5), ("x", 1), ("s", 0),
           ("h", 6), ("h", 7), ("w", 1), ("x", 2), ("s", 1), ("x", 3), ("x", 4), ("s", 2), ("s", 3), ("w", 2),
           ("x", 5), ("s", 4), ("x", 6), ("s", 5), ("x", 7), ("s", 6), ("s", 7), ("w", 3)]
NREL = 2 * WINDOW + 1
ROWS = 4 * DK + 2 * DK


def t5_buckets():
    rel = np.arange(-WINDOW, WINDOW + 1)
    half = N_BUCKETS // 2
    max_exact = half // 2
    n = np.abs(rel)
    n_safe = np.maximum(n, 1).astype(np.float32)
    large = max_exact + (np.log(n_safe / max_exact) / np.log(MAX_DIST / max_exact)
                         * (half - max_exact)).astype(np.int32)
    large = np.minimum(large, half - 1)
    return (rel > 0).astype(np.int32) * half + np.where(n < max_exact, n, large)


def shape_constants():
    s, k = np.arange(SEQ)[:, None], np.arange(NPOS)[None, :]
    turn = 2 * np.pi * ((s * k) % SEQ) / SEQ
    scale = 1.0 / np.sqrt(SEQ * FG_DIM)
    pos = np.concatenate([np.cos(turn) * scale, -np.sin(turn) * scale], axis=1)
    pos = pos.reshape(TB, P, 2 * NPOS).transpose(1, 0, 2).reshape(P, CH_AT)
    c = np.arange(FG_DIM)
    turn = 2 * np.pi * ((c[:, None] * c[None, :]) % FG_DIM) / FG_DIM
    tables = np.concatenate([pos, np.cos(turn), np.sin(turn)], axis=1).astype(np.float32)
    onehot = np.zeros((N_BUCKETS, NREL + 1), np.float32)
    onehot[t5_buckets(), np.arange(NREL)] = 1.0
    return {"tables": tables, "onehot": onehot}


def window(nb):
    blocks = [j for j in (nb - 1, nb, nb + 1) if 0 <= j < TB]
    return blocks, blocks[0] - (nb - 1)


def mixer_schedule():
    steps = [("f", 0), ("f", 1), ("f", 2), ("f", 3), ("channels", 0), ("k",),
             ("positions", 0), ("channels", 1), ("v",), ("positions", 1), ("channels", 2), ("q", 0),
             ("positions", 2), ("channels", 3), ("q", 1), ("positions", 3), ("turn_v",), ("q", 2),
             ("scores", 0, 0), ("scores", 0, 1), ("q", 3), ("scores", 0, 2)]
    queue = []
    for pair in range(DK // 2):
        queue += [("gate_b", pair, i, quarter) for i in range(2) for quarter in range(4)]
        queue += [("branch_b", pair, i, h) for i in range(2) for h in range(2)]
    late = []

    def pieces(n):
        for _ in range(n):
            if not queue:
                return
            piece = queue.pop(0)
            steps.append(piece)
            if piece[0] == "gate_b" and piece[2:] == (1, 3):
                late.append(("sigmoid", piece[1]))
            if piece[0] == "branch_b" and piece[3] == 1:
                late.append(("take_b", piece[1], piece[2]))

    def flush():
        steps.extend(late)
        late.clear()

    units = TB * N_KV
    pieces(1)
    steps += [("scores", 0, 3), ("max", 0), ("exp", 0)]
    pieces(3)
    steps.append(("normalize", 0))
    pieces(1)
    for u in range(units):
        blocks = len(window(u // N_KV)[0])
        more = u + 1 < units
        steps += [("turn", u, 0), ("turn", u, 1)]
        if more:
            steps += [("scores", u + 1, 0), ("scores", u + 1, 1)]
        pieces(1)
        steps.append(("values", u, 0))
        if more:
            steps += [("scores", u + 1, 2), ("scores", u + 1, 3), ("max", u + 1)]
        if blocks == 3:
            steps.append(("turn", u, 2))
        steps.append(("values", u, 1))
        if more:
            steps.append(("exp", u + 1))
        if not any(step[0] == "sigmoid" for step in late):
            flush()
        pieces(1)
        if blocks == 3:
            steps.append(("values", u, 2))
        if more:
            steps.append(("normalize", u + 1))
        pieces(2)
        flush()
        pieces(1 if u % 2 == 0 else 2)
    pieces(len(queue))
    flush()
    return steps


def granule_tiles(g):
    for down in G_DOWN:
        if down <= g < down + SLOTS * DK:
            return DOWN_PARTS[(g - down) % SLOTS]
    if G_B <= g < G_A and (g - G_B) % SLOTS >= 2 or G_A <= g < G_OUT and (g - G_A) % 2:
        return GQ
    return DK


def turn_index(u, b):
    return sum(len(window(v // N_KV)[0]) for v in range(u)) + b


def build(nc, io):
    x, out = io["x"], io["out"]
    w_up = [io["w_up1"][0].rearrange("(k p) n -> p k n", p=P), io["w_up2"][0].rearrange("(k p) n -> p k n", p=P)]
    w_down = [io["w_down1"][0].rearrange("(k p) n -> p k n", p=P), io["w_down2"][0].rearrange("(k p) n -> p k n", p=P)]
    w_in = io["w_in"][0].rearrange("(k p) n -> p k n", p=P)
    w_a = io["w_branch_a"][0]
    w_b = io["w_branch_b"][0].rearrange("(k p) n -> p k n", p=P)
    w_out = io["w_out"][0].rearrange("(k p) n -> p k n", p=P)
    bias_rows = nc.dram_tensor("bias_rows", [N_HEADS, P, SEQ], F32, kind="Internal").ap()
    steps = mixer_schedule()

    with ExitStack() as ctx:
        base = 16512
        at = [base]

        def place(name, shape, dt, offset=None):
            here = at[0] if offset is None else offset
            size = int(np.prod(shape[1:])) * 4
            t = nc.alloc_sbuf_tensor_at(name, shape, dt, offset=here)
            if offset is None:
                at[0] = here + (size + 31) // 32 * 32
            return t, here, (size + 31) // 32 * 32

        xT, _, _ = place("xT", [P, DK * SEQ], F32)
        h_hi, h_at, _ = place("h_hi", [P, DK * SEQ], F32R)
        h_lo, _, _ = place("h_lo", [P, DK * SEQ], F32R)
        raw, _, _ = place("raw", [P, SLOTS, DK, P], F32)
        w_hi, _, _ = place("w_hi", [P, SLOTS, DK, P], F32R)
        w_lo, _, _ = place("w_lo", [P, SLOTS, DK, P], F32R)
        rstd, _, _ = place("rstd", [P, SEQ], F32)
        ident, _, _ = place("ident", [P, P], F32)
        ones, _, _ = place("ones", [P, P], F32)
        ssum, ssum_at, _ = place("ssum", [P, SEQ], F32)
        sq, _, _ = place("sq", [P, 2, SEQ], F32)
        ga_t, _, _ = place("ga_t", [P, SEQ], F32)
        gb_t, _, _ = place("gb_t", [P, SEQ], F32)
        ua_t, ua_at, _ = place("ua_t", [P, SEQ], F32)
        ub_t, _, _ = place("ub_t", [P, SEQ], F32)
        bias_row, br_at, _ = place("bias_row", [N_HEADS, SEQ], F32)
        assert br_at + SEQ * 4 == ua_at + 3 * SEQ * 4
        gate_t, up_t = [ga_t, gb_t], [ua_t, ub_t]
        s_a, _, _ = place("s_a", [P, GQ, 3 * BLK], F32, ssum_at)
        s_b, _, _ = place("s_b", [P, GQ, 3 * BLK], F32, ua_at)
        s_t = [s_a, s_b]
        even_t, _, _ = place("even_t", [P, NPOS], F32)
        y_t, _, _ = place("y_t", [P, SEQ], F32)
        consts, _, _ = place("consts", [P, ROWS], F32)
        rows = y_t
        warm, _, _ = place("warm", [P, 2], F32)
        sink, _, _ = place("sink", [P, N_HEADS], F32)
        half, _, _ = place("half", [P, TB], F32)
        var, _, _ = place("var", [P, TB], F32)
        rinv, _, _ = place("rinv", [P, TB], F32)
        mx, _, _ = place("mx", [P, 2, GQ], F32)
        negm, _, _ = place("negm", [P, 2, GQ], F32)
        sdiff, _, _ = place("sdiff", [P, 2, GQ], F32)
        psumr, _, _ = place("psumr", [P, 2, GQ], F32)
        esink, _, _ = place("esink", [P, 2, GQ], F32)
        den, _, _ = place("den", [P, 2, GQ], F32)
        rden, _, _ = place("rden", [P, 2, GQ], F32)
        a_hi, act_at, a_size = place("a_hi", [P, FK * SEQ], F32R)
        a_lo, _, _ = place("a_lo", [P, FK * SEQ], F32R)
        assert at[0] <= nc.sbuf_usable_end, (at[0], nc.sbuf_usable_end)
        act_end = at[0]
        x_rows, _, xr_size = place("x_rows", [P, TB, D_MODEL], F32, act_at)
        gain_rows, gr_at, gr_size = place("gain_rows", [DK, P], F32, act_at + xr_size)
        table_b, tb_at, tb_size = place("table_b", [N_BUCKETS, N_HEADS], F32, gr_at + gr_size)
        onehot, _, _ = place("onehot", [N_BUCKETS, NREL + 1], F32, tb_at + tb_size)
        here = [act_at]

        def reuse(name, shape, dt):
            t, where, size = place(name, shape, dt, here[0])
            here[0] += size
            assert here[0] <= act_end
            return t, where

        kp_hi, _ = reuse("kp_hi", [P, N_KV, SEQ], F32R)
        kp_lo, _ = reuse("kp_lo", [P, N_KV, SEQ], F32R)
        v_hi, _ = reuse("v_hi", [P, TB, P], F32R)
        v_lo, _ = reuse("v_lo", [P, TB, P], F32R)
        bias, bias_at = reuse("bias", [P, N_HEADS, 3 * BLK], F32)
        ab_hi, ab_at = reuse("ab_hi", [P, TB, 2 * FG_DIM], F32R)
        ab_lo, _ = reuse("ab_lo", [P, TB, 2 * FG_DIM], F32R)
        assert here[0] - act_at == 2 * DK * SEQ * 4
        tab_hi, tab_at = reuse("tab_hi", [P, TABLE], F32R)
        tab_lo, _ = reuse("tab_lo", [P, TABLE], F32R)
        qo_hi, _ = reuse("qo_hi", [P, GQ, SEQ], F32R)
        qo_lo, _ = reuse("qo_lo", [P, GQ, SEQ], F32R)
        fy_hi, _ = reuse("fy_hi", [P, N_FGROUPS, SEQ], F32R)
        fy_lo, _ = reuse("fy_lo", [P, N_FGROUPS, SEQ], F32R)
        tab_raw, _, _ = place("tab_raw", [P, TABLE], F32, bias_at)
        pt_hi, pt_at, pt_size = place("pt_hi", [P, 2, GQ * BLK], F32R, ab_at)
        pt_lo, _, _ = place("pt_lo", [P, 2, GQ * BLK], F32R, ab_at + pt_size)
        mix_b, _, _ = place("mix_b", [P, DK * SEQ], F32, tab_at)
        m_hi, _, m_size = place("m_hi", [P, DK * SEQ], F32R, act_at)
        m_lo, _, _ = place("m_lo", [P, DK * SEQ], F32R, act_at + m_size)
        y_rows, _, _ = place("y_rows", [P, TB, D_MODEL], F32, h_at)

        banks = [ctx.enter_context(nc.psum_tensor(f"bank{i}", [P, SEQ], F32)) for i in range(8)]

        def sem(name):
            return ctx.enter_context(nc.semaphore(name))

        x_landed = [sem(f"x_landed{i}") for i in range(4)]
        gain_landed = sem("gain_landed")
        rows_landed, buckets_landed, sink_landed = sem("rows_landed"), sem("buckets_landed"), sem("sink_landed")
        raw_landed = [sem(f"raw_landed{i}") for i in range(SLOTS)]
        q_second, a_second = [sem(f"q_second{i}") for i in range(GQ)], [sem(f"a_second{i}") for i in range(2)]
        bias_stored, bias_landed, tables_landed = sem("bias_stored"), sem("bias_landed"), sem("tables_landed")
        out_stored = sem("out_stored")
        ident_ready, fills_ready = sem("ident_ready"), sem("fills_ready")
        sum_added, rinv_ready, zeros_ready = sem("sum_added"), sem("rinv_ready"), sem("zeros_ready")
        w_hi_ready, h_hi_ready, sq_ready = sem("w_hi_ready"), sem("h_hi_ready"), sem("sq_ready")
        silu_ready, a_hi_ready, gate_ready = sem("silu_ready"), sem("a_hi_ready"), sem("gate_ready")
        proj_hi_ready, tab_hi_ready, exp_ready = sem("proj_hi_ready"), sem("tab_hi_ready"), sem("exp_ready")
        pt_hi_ready, o_hi_ready, ab_hi_ready = sem("pt_hi_ready"), sem("o_hi_ready"), sem("ab_hi_ready")
        even_copied, y_hi_ready, m_hi_ready = sem("even_copied"), sem("y_hi_ready"), sem("m_hi_ready")
        y_rows_ready, scaled_act = sem("y_rows_ready"), sem("scaled_act")
        w_lo_ready, h_lo_ready, x_ready = sem("w_lo_ready"), sem("h_lo_ready"), sem("x_ready")
        out_read, product_ready, a_lo_ready = sem("out_read"), sem("product_ready"), sem("a_lo_ready")
        gain_ready, consts_ready, row_ready = sem("gain_ready"), sem("consts_ready"), sem("row_ready")
        var_ready, diag_ready, rstd_ready = sem("var_ready"), sem("diag_ready"), sem("rstd_ready")
        proj_lo_ready, v_lo_ready, tab_lo_ready = sem("proj_lo_ready"), sem("v_lo_ready"), sem("tab_lo_ready")
        v_hi_ready = sem("v_hi_ready")
        s_read, max_ready, den_ready, probs_ready = sem("s_read"), sem("max_ready"), sem("den_ready"), sem("probs_ready")
        pt_lo_ready, o_lo_ready, ab_lo_ready = sem("pt_lo_ready"), sem("o_lo_ready"), sem("ab_lo_ready")
        y_ready, y_lo_ready = sem("y_ready"), sem("y_lo_ready")
        mixed, m_lo_ready, scaled_dve = sem("mixed"), sem("m_lo_ready"), sem("scaled_dve")
        w_used, turned, bias_done = sem("w_used"), sem("turned"), sem("bias_done")
        gain_turned, consts_turned = sem("gain_turned"), sem("consts_turned")
        sum_done, rstd_done, v_turned = sem("sum_done"), sem("rstd_done"), sem("v_turned")
        s_done, pt_done, o_done = sem("s_done"), sem("pt_done"), sem("o_done")
        pt_used = sem("pt_used")
        ab_done, even_done, odd_done, y_turned = sem("ab_done"), sem("even_done"), sem("odd_done"), sem("y_turned")

        block = ctx.enter_context(nc.Block())

        def tile(t, m):
            if isinstance(m, int):
                return t[:, m * SEQ:(m + 1) * SEQ]
            return t[:, bass.ds(m * SEQ, SEQ)]

        def x_bank(m):
            return 8 - X_BANKS + m % X_BANKS

        def gain(n, m):
            if isinstance(m, int):
                return consts[:, n * DK + m:n * DK + m + 1]
            return consts[:, bass.ds(m + n * DK, 1)]


        @block.sync
        def _(sp):
            def load(g, dst, src, it=0, n=0):
                if g >= SLOTS or n:
                    sp.wait_ge(w_lo_ready, g - SLOTS + 1 + n * it)
                sp.dma_start(dst, src).then_inc(raw_landed[g % SLOTS], 16)

            def up(r, it, j, n=0):
                g = G_UP[r] + j
                col = it * (2 * P) + (j // 2) * P + (j % 2) * D_FF
                cols = slice(col, col + P) if isinstance(it, int) else bass.ds(sp.snap(col), P)
                load(g, raw[:, g % SLOTS, :, :], w_up[r][:, :, cols], it, n)

            def down(r, m, j, n=0):
                g = G_DOWN[r] + j
                k0, nk = DOWN_AT[j], DOWN_PARTS[j]
                load(g, raw[:, g % SLOTS, 0:nk, :], w_down[r][:, k0:k0 + nk, bass.ds(sp.snap(m * P), P)], m, n)

            xv = x[0].rearrange("(t p) d -> p t d", p=P)
            for c in range(4):
                w = D_MODEL // 4
                sp.dma_start(x_rows[:, :, c * w:(c + 1) * w], xv[:, :, c * w:(c + 1) * w]).then_inc(x_landed[c], 16)
                if c == 0:
                    up(0, 0, 0)
            for r in range(2):
                if r == 0:
                    for j in range(1, SLOTS):
                        up(0, 0, j)
                    r0 = 0
                    for name, nr in (("g_mix", DK), ("g_ffn2", DK), ("g_final", DK), ("b_gate", 2 * DK)):
                        v = io[name] if name == "g_final" else io[name][0]
                        sp.dma_start(rows[r0:r0 + nr, 0:P], v.rearrange("(r p) -> r p", p=P)).then_inc(rows_landed, 16)
                        r0 += nr
                    sp.dma_start(table_b[:, :], io["rel_bias"]).then_inc(buckets_landed, 16)
                    sp.dma_start(onehot[:, :], io["onehot"]).then_inc(buckets_landed, 16)
                    sp.dma_start(sink[:, :], io["sink"].broadcast_to([P, N_HEADS])).then_inc(sink_landed, 16)
                with sp.Fori(1 - r, FK // 2) as it:
                    for j in range(SLOTS):
                        up(r, it, j, SLOTS)
                with sp.Fori(0, DK) as m:
                    for j in range(SLOTS):
                        down(r, m, j, SLOTS)
                if r == 1:
                    break
                for c in range(N_FGROUPS):
                    g, col = G_F + c, Q_WIDTH + 2 * KV_WIDTH + c * FG_DIM
                    load(g, raw[:, g % SLOTS, :, :], w_in[:, :, col:col + P])
                for g, col in ((G_K, Q_WIDTH), (G_V, Q_WIDTH + KV_WIDTH)):
                    load(g, raw[:, g % SLOTS, :, :], w_in[:, :, col:col + P])
                q_cols = w_in[:, :, 0:Q_WIDTH].rearrange("p k (v c d) -> p k v c d", v=N_KV, c=GQ)
                for c in range(GQ):
                    g = G_Q + c
                    load(g, raw[:, g % SLOTS, :, 0:HD], q_cols[:, :, 0, c, :])
                    sp.dma_start(raw[:, g % SLOTS, :, HD:P], q_cols[:, :, 1, c, :]).then_inc(q_second[c], 16)
                gates_at = Q_WIDTH + 2 * KV_WIDTH + F_WIDTH
                for pair in range(DK // 2):
                    g0 = G_B + SLOTS * pair
                    for i in range(2):
                        col = gates_at + D_MODEL + (2 * pair + i) * P
                        load(g0 + i, raw[:, (g0 + i) % SLOTS, :, :], w_in[:, :, col:col + P])
                    for i in range(2):
                        g, col = g0 + 2 + i, (2 * pair + i) * P
                        load(g, raw[:, g % SLOTS, 0:N_FGROUPS, :], w_b[:, :, col:col + P])
                wa_v = w_a.rearrange("(v c d) n -> v d c n", v=N_KV, c=GQ)
                with sp.Fori(0, DK // 2) as pair:
                    for i in range(2):
                        g = G_A + 2 * i
                        cols = bass.ds(sp.snap(pair * (2 * P) + (gates_at + i * P)), P)
                        load(g, raw[:, g % SLOTS, :, :], w_in[:, :, cols], pair, SLOTS)
                        g = G_A + 2 * i + 1
                        cols = bass.ds(sp.snap(pair * (2 * P) + i * P), P)
                        load(g, raw[HD:P, g % SLOTS, 0:GQ, :], wa_v[1, :, :, cols], pair, SLOTS)
                        sp.dma_start(raw[0:HD, g % SLOTS, 0:GQ, :], wa_v[0, :, :, cols]).then_inc(a_second[i], 16)
                with sp.Fori(0, DK // SLOTS) as it:
                    for j in range(SLOTS):
                        g = G_OUT + j
                        load(g, raw[:, g % SLOTS, :, :], w_out[:, :, bass.ds(sp.snap(it * (SLOTS * P) + j * P), P)], it, SLOTS)
            ov = out[0].rearrange("(t p) d -> p t d", p=P)
            for t in range(TB):
                if t % 2:
                    sp.wait_ge(scaled_act, t // 2 + 1)
                else:
                    sp.wait_ge(scaled_dve, t // 2 + 1)
                sp.dma_start(ov[:, t, :], y_rows[:, t, :]).then_inc(out_stored, 16)
            sp.wait_ge(out_stored, 16 * TB)

        @block.scalar
        def _(act):
            def copy(dst, src, scale=1.0):
                return nc.scalar.activation(dst, src, ACT.Copy, scale=scale)

            def split_hi(g, it=0, n=0):
                s, static = g % SLOTS, isinstance(it, int)
                nk = granule_tiles(g + n * it if static else g)
                act.wait_ge(raw_landed[s], 16 * (g // SLOTS + 1) + 4 * n * it)
                if static and G_Q <= g + n * it < G_Q + GQ:
                    act.wait_ge(q_second[g + n * it - G_Q], 16)
                at_a = g - G_A if not static or n == 0 else g + n * it - G_A
                if 0 <= at_a < 2 * DK and at_a % 2:
                    turn_ = at_a // SLOTS + (0 if static else it)
                    act.wait_ge(a_second[at_a % SLOTS // 2], 16 * turn_ + 16)
                if g >= SLOTS:
                    act.wait_ge(w_used, g - SLOTS + 1 + n * it)
                copy(w_hi[:, s, 0:nk, :], raw[:, s, 0:nk, :]).then_inc(w_hi_ready, 1)

            def square_free(n, m):
                if not isinstance(m, int) or m >= 3:
                    act.wait_ge(sum_added, m + ((DK - 1) * n - 2))

            def residual(n, m, odd, first=False):
                if n < NORM_FINAL:
                    copy(tile(h_hi, m), tile(xT, m), scale=gain(n, m)).then_inc(h_hi_ready, 1)
                else:
                    copy(gate_t[odd][:, :], tile(xT, m), scale=gain(n, m)).then_inc(h_hi_ready, 1)
                square(tile(xT, m), odd, first)

            def square(src, odd, first):
                nc.scalar.activation(ssum[:, :] if first else sq[:, odd, :], src, ACT.Square).then_inc(sq_ready, 1)

            act.dma_start(gain_rows[:, :], io["g_ffn1"][0].rearrange("(r p) -> r p", p=P)).then_inc(gain_landed, 16)
            act.wait_ge(fills_ready, 1)
            nc.scalar.activation(warm[:, :], ones[:, 0:2], ACT.Silu)
            act.wait_ge(gain_ready, 1)

            def x_hi(m):
                act.wait_ge(turned, m + 1)
                copy(tile(h_hi, m), banks[x_bank(m)][:, :], scale=gain(NORM_FFN1, m)).then_inc(h_hi_ready, 1)

            def x_square(m):
                act.wait_ge(x_ready, m + 1)
                square_free(NORM_FFN1, m)
                square(tile(xT, m), m % 2, m == 0)

            for piece in X_ORDER:
                if piece[0] == "h":
                    x_hi(piece[1])
                elif piece[0] == "s":
                    x_square(piece[1])
                elif piece[0] == "w":
                    split_hi(piece[1])

            def ffn_up(r, it, n=SLOTS):
                for j in range(2):
                    g, o = G_UP[r] + 2 * j, O_UP[r] + 2 * j
                    split_hi(g + SLOTS, it, n)
                    act.wait_ge(out_read, o + 1 + n * it)
                    nc.scalar.activation(gate_t[j][:, :], gate_t[j][:, :], ACT.Silu).then_inc(silu_ready, 1)
                    split_hi(g + 1 + SLOTS, it, n)
                    act.wait_ge(product_ready, FK * r + j + 1 + 2 * it)
                    copy(tile(a_hi, 2 * it + j), up_t[j][:, :]).then_inc(a_hi_ready, 1)

            def turned_rows(m, odd):
                act.wait_ge(y_turned, m + 1)
                dst = y_rows[:, :, m * P:(m + 1) * P] if isinstance(m, int) else y_rows[:, :, bass.ds(m * P, P)]
                copy(dst, banks[6 + odd][:, :].rearrange("p (t d) -> p t d", t=TB)).then_inc(y_rows_ready, 1)

            def ffn_down(r, it, first=False, last=False, n=2 * SLOTS):
                for j in range(2):
                    g, m = G_DOWN[r] + SLOTS * j, 2 * it + j
                    ahead = not (r == 1 and last and j == 1)
                    if ahead:
                        for i in range(3):
                            split_hi(g + SLOTS + i, it, n)
                    if r == 1 and not (first and j == 0):
                        turned_rows(m - 1, 1 - j)
                    nrm = NORM_MIX if r == 0 else NORM_FINAL
                    square_free(nrm, m)
                    act.wait_ge(out_read, O_DOWN[r] + j + 1 + 2 * it)
                    residual(nrm, m, j, first and j == 0)
                    if ahead:
                        split_hi(g + SLOTS + 3, it, n)

            for r in range(2):
                with act.Fori(0, FK // 2 - 1) as it:
                    ffn_up(r, it)
                ffn_up(r, FK // 2 - 1)
                if r == 0:
                    act.wait_ge(consts_ready, 1)
                    act.wait_ge(row_ready, 1)
                    act.dma_start(bias_rows, bias_row[:, :].unsqueeze(1).broadcast_to([N_HEADS, P, SEQ])
                                  ).then_inc(bias_stored, 16)
                ffn_down(r, 0, first=True)
                with act.Fori(1, DK // 2 - 1) as it:
                    ffn_down(r, it)
                ffn_down(r, DK // 2 - 1, last=True)
                if r == 1:
                    break

                act.dma_start(tab_raw[:, :], io["tables"]).then_inc(tables_landed, 16)
                for step in steps:
                    kind = step[0]
                    if kind == "f":
                        grp = step[1]
                        split_hi(G_F + grp + SLOTS)
                        act.wait_ge(out_read, O_F + grp + 1)
                        copy(fy_hi[:, grp, :], gate_t[grp % 2][:, :]).then_inc(proj_hi_ready, 1)
                        if grp == 1:
                            act.wait_ge(tables_landed, 16)
                            copy(tab_hi[:, :], tab_raw[:, :]).then_inc(tab_hi_ready, 1)
                    elif kind == "k":
                        split_hi(G_K + SLOTS)
                        act.wait_ge(zeros_ready, 2)
                        act.wait_ge(out_read, O_K + 1)
                        for v in range(N_KV):
                            rows_v = slice(v * HD, (v + 1) * HD)
                            last = copy(kp_hi[rows_v, v, :], ga_t[rows_v, :])
                        last.then_inc(proj_hi_ready, 1)
                        act.wait_ge(tab_lo_ready, 1)
                        act.wait_ge(bias_stored, 16)
                        diagonals = bias_rows.rearrange("h q m -> h (q m)")[:, BLK - 1:BLK - 1 + P * (SEQ - 1)]
                        diagonals = diagonals.rearrange("h (q m) -> q h m", m=SEQ - 1)[:, :, 0:3 * BLK]
                        act.dma_start(bias[:, :, :], diagonals).then_inc(bias_landed, 16)
                    elif kind == "v":
                        split_hi(G_V + SLOTS)
                    elif kind == "q":
                        c = step[1]
                        split_hi(G_Q + c + SLOTS)
                        act.wait_ge(out_read, O_Q + c + 1)
                        copy(qo_hi[:, c, :], gate_t[(c + 1) % 2][:, :]).then_inc(proj_hi_ready, 1)
                    elif kind == "turn_v":
                        act.wait_ge(v_turned, 1)
                        copy(v_hi[:, :, :], banks[B_CH][:, :]).then_inc(v_hi_ready, 1)
                    elif kind == "channels":
                        grp = step[1]
                        for i in range(2):
                            act.wait_ge(ab_done, 2 * grp + i + 1)
                            copy(ab_hi[:, 2 * i:2 * i + 2, :], banks[B_CH + i][:, :]).then_inc(ab_hi_ready, 1)
                    elif kind == "positions":
                        grp = step[1]
                        act.wait_ge(even_done, grp + 1)
                        if grp:
                            act.wait_ge(y_ready, 2 * grp)
                        copy(even_t[:, :], banks[B_POS][:, 0:NPOS]).then_inc(even_copied, 1)
                        act.wait_ge(y_ready, 2 * grp + 2)
                        copy(fy_hi[:, grp, :], y_t[:, :]).then_inc(y_hi_ready, 1)
                    elif kind == "exp":
                        u = step[1]
                        width = len(window(u // N_KV)[0]) * BLK
                        act.wait_ge(max_ready, 3 * u + 3)
                        for c in range(GQ):
                            sc = s_t[u % 2][:, c, 0:width]
                            nc.scalar.activation(sc, sc, ACT.Exp, bias=negm[:, u % 2, c:c + 1],
                                                 accum_out=psumr[:, u % 2, c:c + 1])
                        nc.scalar.activation(esink[:, u % 2, :], sdiff[:, u % 2, :], ACT.Exp).then_inc(exp_ready, 1)
                    elif kind == "turn":
                        t = turn_index(*step[1:])
                        act.wait_ge(pt_done, t + 1)
                        if t >= 2:
                            act.wait_ge(pt_used, t - 1)
                        copy(pt_hi[:, t % 2, :], banks[B_PT[t % 2]][:, :]).then_inc(pt_hi_ready, 1)
                    elif kind == "values":
                        u, b = step[1:]
                        nb, kv = u // N_KV, u % N_KV
                        if b == len(window(nb)[0]) - 1:
                            rows_v = slice(kv * HD, (kv + 1) * HD)
                            act.wait_ge(pt_used, turn_index(u, b) + 1)
                            copy(qo_hi[rows_v, :, nb * BLK:(nb + 1) * BLK],
                                 banks[B_O[u % 2]][rows_v, :].rearrange("p (c q) -> p c q", c=GQ)
                                 ).then_inc(o_hi_ready, 1)
                    elif kind == "gate_b" and step[3] == 3:
                        split_hi(G_B + SLOTS * step[1] + step[2] + SLOTS)
                    elif kind == "sigmoid":
                        pair = step[1]
                        for i in range(2):
                            b = 5 * DK + 2 * pair + i
                            act.wait_ge(out_read, O_B + SLOTS * pair + i + 1)
                            nc.scalar.activation(gate_t[i][:, :], gate_t[i][:, :], ACT.Sigmoid,
                                                 bias=consts[:, b:b + 1]).then_inc(gate_ready, 1)
                    elif kind == "branch_b" and step[3] == 1:
                        split_hi(G_B + SLOTS * step[1] + 2 + step[2] + SLOTS)

                def mix(pair, n=SLOTS):
                    for i in range(2):
                        m = 2 * pair + i
                        split_hi(G_A + 2 * i + SLOTS, pair, n)
                        act.wait_ge(out_read, O_A + 2 * i + 1 + n * pair)
                        b = 4 * DK
                        b_gate = consts[:, b + m:b + m + 1] if isinstance(m, int) else consts[:, bass.ds(m + b, 1)]
                        nc.scalar.activation(gate_t[i][:, :], gate_t[i][:, :], ACT.Sigmoid,
                                             bias=b_gate).then_inc(gate_ready, 1)
                        split_hi(G_A + 2 * i + 1 + SLOTS, pair, n)
                        act.wait_ge(mixed, m + 1)
                        copy(tile(m_hi, m), up_t[i][:, :]).then_inc(m_hi_ready, 1)

                with act.Fori(0, DK // 2 - 1) as pair:
                    mix(pair)
                mix(DK // 2 - 1)
                for m in range(DK):
                    split_hi(G_OUT + m + SLOTS)
                    square_free(NORM_FFN2, m)
                    act.wait_ge(out_read, O_OUT + m + 1)
                    residual(NORM_FFN2, m, m % 2, m == 0)

            turned_rows(DK - 1, 1)
            act.wait_ge(rinv_ready, NORM_FINAL + 1)
            act.wait_ge(y_rows_ready, DK)
            for t in range(1, TB, 2):
                copy(y_rows[:, t, :], y_rows[:, t, :], scale=rinv[:, t:t + 1]).then_inc(scaled_act, 1)

        @block.vector
        def _(dve):
            vec = nc.vector

            def split_lo(g, it=0, n=0):
                s = g % SLOTS
                nk = granule_tiles(g + n * it if isinstance(it, int) else g)
                dve.wait_ge(w_hi_ready, g + 1 + n * it)
                vec.tensor_tensor(w_lo[:, s, 0:nk, :], raw[:, s, 0:nk, :], w_hi[:, s, 0:nk, :].bitcast(F32),
                                  ALU.subtract).then_inc(w_lo_ready, 1)

            def lo(dst, full, hi):
                return vec.tensor_tensor(dst, full, hi.bitcast(F32), ALU.subtract)

            def new_h_lo(n, m):
                dve.wait_ge(h_hi_ready, m + (DK * n + 1))
                vec.scalar_tensor_tensor(out=tile(h_lo, m), in0=tile(xT, m), scalar=gain(n, m),
                                         in1=tile(h_hi, m).bitcast(F32), op0=ALU.mult,
                                         op1=ALU.subtract).then_inc(h_lo_ready, 1)

            def norm_factors(n):
                mean(n)
                dve.wait_ge(rinv_ready, n + 1)
                for t in range(TB):
                    last = vec.tensor_scalar(gb_t[:, t * P:(t + 1) * P], ident[:, :], rinv[:, t:t + 1], None, ALU.mult)
                last.then_inc(diag_ready, 1)
                dve.wait_ge(rstd_done, n + 1)
                vec.tensor_copy(rstd[:, :], banks[B_RSTD][:, :]).then_inc(rstd_ready, 1)
                dve.wait_ge(rstd_ready, n + 1)

            def mean(n):
                dve.wait_ge(sum_done, n + 1)
                vec.tensor_scalar(var[:, :], banks[B_SUM][:, 0:2 * TB:2], 1.0 / D_MODEL, EPS, ALU.mult,
                                  ALU.add).then_inc(var_ready, 1)

            dve.wait_ge(gain_turned, 1)
            vec.tensor_copy(consts[:, 0:DK], banks[0][:, 0:DK]).then_inc(gain_ready, 1)
            dve.wait_ge(gain_ready, 1)
            for piece in X_ORDER:
                m = piece[1]
                if piece[0] == "h":
                    dve.wait_ge(h_hi_ready, m + 1)
                    vec.scalar_tensor_tensor(out=tile(h_lo, m), in0=banks[x_bank(m)][:, :], scalar=gain(NORM_FFN1, m),
                                             in1=tile(h_hi, m).bitcast(F32), op0=ALU.mult,
                                             op1=ALU.subtract).then_inc(h_lo_ready, 1)
                elif piece[0] == "x":
                    vec.tensor_copy(tile(xT, m), banks[x_bank(m)][:, :]).then_inc(x_ready, 1)
                elif piece[0] == "w":
                    split_lo(m)
            def ffn_up(r, it, first=False, n=SLOTS):
                for j in range(2):
                    g, o, f = G_UP[r] + 2 * j, O_UP[r] + 2 * j, FK * r + j
                    split_lo(g + SLOTS, it, n)
                    if first and j == 0:
                        norm_factors(NORM_FFN1 if r == 0 else NORM_FFN2)
                    dve.wait_ge(w_used, g + 1 + n * it)
                    vec.tensor_tensor(gate_t[j][:, :], banks[o % BANKS][:, :], rstd[:, :], ALU.mult).then_inc(out_read, 1)
                    split_lo(g + 1 + SLOTS, it, n)
                    dve.wait_ge(w_used, g + 2 + n * it)
                    vec.tensor_tensor(up_t[j][:, :], banks[(o + 1) % BANKS][:, :], rstd[:, :], ALU.mult).then_inc(out_read, 1)
                    dve.wait_ge(out_read, o + 2 + n * it)
                    dve.wait_ge(silu_ready, f + 1 + 2 * it)
                    vec.tensor_tensor(up_t[j][:, :], gate_t[j][:, :], up_t[j][:, :], ALU.mult).then_inc(product_ready, 1)
                    dve.wait_ge(a_hi_ready, f + 1 + 2 * it)
                    lo(tile(a_lo, 2 * it + j), up_t[j][:, :], tile(a_hi, 2 * it + j)).then_inc(a_lo_ready, 1)

            def residual(n, m, o, scale, it=0, per=0):
                vec.scalar_tensor_tensor(out=tile(xT, m), in0=banks[o % BANKS][:, :], scalar=scale, in1=tile(xT, m),
                                         op0=ALU.mult, op1=ALU.add).then_inc(out_read, 1)

            def ffn_down(r, it, last=False, n=2 * SLOTS):
                nrm = NORM_MIX if r == 0 else NORM_FINAL
                for j in range(2):
                    g, o, m = G_DOWN[r] + SLOTS * j, O_DOWN[r] + j, 2 * it + j
                    ahead = not (r == 1 and last and j == 1)
                    if ahead:
                        for i in range(3):
                            split_lo(g + SLOTS + i, it, n)
                    dve.wait_ge(w_used, g + SLOTS + n * it)
                    residual(nrm, m, o, 0.5)
                    if nrm < NORM_FINAL:
                        dve.wait_ge(out_read, o + 1 + 2 * it)
                        new_h_lo(nrm, m)
                    if ahead:
                        split_lo(g + SLOTS + 3, it, n)

            for r in range(2):
                ffn_up(r, 0, first=True)
                if r == 0:
                    dve.wait_ge(consts_turned, 1)
                    vec.tensor_copy(consts[:, DK:ROWS], banks[6][:, 0:ROWS - DK]).then_inc(consts_ready, 1)
                    dve.wait_ge(fills_ready, 3)
                    dve.wait_ge(bias_done, 1)
                    vec.tensor_copy(bias_row[:, P - 1:P - 1 + NREL], banks[7][0:N_HEADS, 0:NREL]).then_inc(row_ready, 1)
                with dve.Fori(1, FK // 2 - 1) as it:
                    ffn_up(r, it)
                ffn_up(r, FK // 2 - 1)
                with dve.Fori(0, DK // 2 - 1) as it:
                    ffn_down(r, it)
                ffn_down(r, DK // 2 - 1, last=True)
                if r == 1:
                    break

                for step in steps:
                    kind = step[0]
                    if kind == "f":
                        grp = step[1]
                        split_lo(G_F + grp + SLOTS)
                        if grp == 0:
                            norm_factors(NORM_MIX)
                        dve.wait_ge(w_used, G_F + grp + 1)
                        vec.tensor_tensor(gate_t[grp % 2][:, :], banks[(O_F + grp) % BANKS][:, :], rstd[:, :],
                                          ALU.mult).then_inc(out_read, 1)
                        dve.wait_ge(proj_hi_ready, grp + 1)
                        lo(fy_lo[:, grp, :], gate_t[grp % 2][:, :], fy_hi[:, grp, :]).then_inc(proj_lo_ready, 1)
                        if grp == 1:
                            dve.wait_ge(tab_hi_ready, 1)
                            lo(tab_lo[:, :], tab_raw[:, :], tab_hi[:, :]).then_inc(tab_lo_ready, 1)
                    elif kind == "k":
                        split_lo(G_K + SLOTS)
                        dve.wait_ge(w_used, G_K + 1)
                        vec.tensor_tensor(ga_t[:, :], banks[O_K % BANKS][:, :], rstd[:, :], ALU.mult).then_inc(out_read, 1)
                        dve.wait_ge(proj_hi_ready, N_FGROUPS + 1)
                        for v in range(N_KV):
                            rows_v = slice(v * HD, (v + 1) * HD)
                            last = lo(kp_lo[rows_v, v, :], ga_t[rows_v, :], kp_hi[rows_v, v, :])
                        last.then_inc(proj_lo_ready, 1)
                    elif kind == "v":
                        split_lo(G_V + SLOTS)
                        dve.wait_ge(w_used, G_V + 1)
                        vec.tensor_tensor(ua_t[:, :], banks[O_V % BANKS][:, :], rstd[:, :], ALU.mult).then_inc(out_read, 1)
                    elif kind == "q":
                        c = step[1]
                        split_lo(G_Q + c + SLOTS)
                        dve.wait_ge(w_used, G_Q + c + 1)
                        q_t = gate_t[(c + 1) % 2]
                        vec.scalar_tensor_tensor(out=q_t[:, :], in0=banks[(O_Q + c) % BANKS][:, :], scalar=HD ** -0.5,
                                                 in1=rstd[:, :], op0=ALU.mult, op1=ALU.mult).then_inc(out_read, 1)
                        dve.wait_ge(proj_hi_ready, N_FGROUPS + 2 + c)
                        lo(qo_lo[:, c, :], q_t[:, :], qo_hi[:, c, :]).then_inc(proj_lo_ready, 1)
                    elif kind == "turn_v":
                        dve.wait_ge(v_hi_ready, 1)
                        lo(v_lo[:, :, :], banks[B_CH][:, :].rearrange("p (t d) -> p t d", t=TB),
                           v_hi[:, :, :]).then_inc(v_lo_ready, 1)
                    elif kind == "channels":
                        grp = step[1]
                        for i in range(2):
                            dve.wait_ge(ab_hi_ready, 2 * grp + i + 1)
                            lo(ab_lo[:, 2 * i:2 * i + 2, :],
                               banks[B_CH + i][:, :].rearrange("p (t d) -> p t d", t=2),
                               ab_hi[:, 2 * i:2 * i + 2, :]).then_inc(ab_lo_ready, 1)
                    elif kind == "positions":
                        grp, h = step[1], SEQ // 2
                        dve.wait_ge(odd_done, grp + 1)
                        dve.wait_ge(even_copied, grp + 1)
                        vec.tensor_tensor(y_t[:, 0:h + 1], even_t[:, 0:h + 1], banks[B_POS + 1][:, 0:h + 1],
                                          ALU.add).then_inc(y_ready, 1)
                        vec.tensor_tensor(y_t[:, SEQ - 1:h:-1], even_t[:, 1:h], banks[B_POS + 1][:, 1:h],
                                          ALU.subtract).then_inc(y_ready, 1)
                        dve.wait_ge(y_hi_ready, grp + 1)
                        lo(fy_lo[:, grp, :], y_t[:, :], fy_hi[:, grp, :]).then_inc(y_lo_ready, 1)
                    elif kind == "scores":
                        u, c = step[1:]
                        nb, kv, b = u // N_KV, u % N_KV, u % 2
                        blocks, w0 = window(nb)
                        width = len(blocks) * BLK
                        if u == 0 and c == 0:
                            dve.wait_ge(bias_landed, 16)
                            dve.wait_ge(sink_landed, 16)
                        dve.wait_ge(s_done, GQ * u + c + 1)
                        vec.tensor_tensor_reduce(
                            out=s_t[b][:, c, 0:width], in0=banks[B_S + c % 2][:, 0:width],
                            in1=bias[:, GQ * kv + c, w0 * BLK:w0 * BLK + width], scale=1.0, scalar=NEG,
                            op0=ALU.add, op1=ALU.max, accum_out=mx[:, b, c:c + 1]).then_inc(s_read, 1)
                    elif kind == "max":
                        u = step[1]
                        b, kv = u % 2, u % N_KV
                        sk = sink[:, GQ * kv:GQ * (kv + 1)]
                        dve.wait_ge(s_read, GQ * (u + 1))
                        vec.tensor_tensor(mx[:, b, :], mx[:, b, :], sk, ALU.max).then_inc(max_ready, 1)
                        dve.wait_ge(max_ready, 3 * u + 1)
                        vec.tensor_scalar(negm[:, b, :], mx[:, b, :], -1.0, None, ALU.mult).then_inc(max_ready, 1)
                        vec.tensor_tensor(sdiff[:, b, :], sk, mx[:, b, :], ALU.subtract).then_inc(max_ready, 1)
                    elif kind == "normalize":
                        u = step[1]
                        b = u % 2
                        width = len(window(u // N_KV)[0]) * BLK
                        dve.wait_ge(exp_ready, u + 1)
                        vec.tensor_tensor(den[:, b, :], psumr[:, b, :], esink[:, b, :], ALU.add).then_inc(den_ready, 1)
                        dve.wait_ge(den_ready, 2 * u + 1)
                        vec.reciprocal(rden[:, b, :], den[:, b, :]).then_inc(den_ready, 1)
                        dve.wait_ge(den_ready, 2 * u + 2)
                        for c in range(GQ):
                            sc = s_t[b][:, c, 0:width]
                            last = vec.tensor_scalar(sc, sc, rden[:, b, c:c + 1], None, ALU.mult)
                        last.then_inc(probs_ready, 1)
                    elif kind == "turn":
                        t = turn_index(*step[1:])
                        dve.wait_ge(pt_hi_ready, t + 1)
                        lo(pt_lo[:, t % 2, :], banks[B_PT[t % 2]][:, :], pt_hi[:, t % 2, :]).then_inc(pt_lo_ready, 1)
                    elif kind == "values":
                        u, b = step[1:]
                        nb, kv = u // N_KV, u % N_KV
                        if b == len(window(nb)[0]) - 1:
                            rows_v, cols = slice(kv * HD, (kv + 1) * HD), slice(nb * BLK, (nb + 1) * BLK)
                            dve.wait_ge(o_hi_ready, u + 1)
                            lo(qo_lo[rows_v, :, cols],
                               banks[B_O[u % 2]][rows_v, :].rearrange("p (c q) -> p c q", c=GQ),
                               qo_hi[rows_v, :, cols]).then_inc(o_lo_ready, 1)
                    elif kind == "gate_b" and step[3] == 3:
                        g, i = G_B + SLOTS * step[1] + step[2], step[2]
                        split_lo(g + SLOTS)
                        dve.wait_ge(w_used, g + 1)
                        vec.tensor_tensor(gate_t[i][:, :], banks[i][:, :], rstd[:, :], ALU.mult).then_inc(out_read, 1)
                    elif kind == "branch_b" and step[3] == 1:
                        pair, i = step[1:3]
                        split_lo(G_B + SLOTS * pair + 2 + i + SLOTS)
                    elif kind == "take_b":
                        pair, i = step[1:]
                        dve.wait_ge(w_used, G_B + SLOTS * pair + 2 + i + 1)
                        dve.wait_ge(gate_ready, 2 * pair + i + 1)
                        vec.tensor_tensor(tile(mix_b, 2 * pair + i), banks[i][:, :], gate_t[i][:, :],
                                          ALU.mult).then_inc(out_read, 1)

                def mix(pair, n=SLOTS):
                    for i in range(2):
                        m, g, o = 2 * pair + i, G_A + 2 * i, O_A + 2 * i
                        split_lo(g + SLOTS, pair, n)
                        dve.wait_ge(out_read, o - 1 + n * pair)
                        dve.wait_ge(w_used, g + 1 + n * pair)
                        vec.tensor_tensor(gate_t[i][:, :], banks[o % BANKS][:, :], rstd[:, :], ALU.mult).then_inc(out_read, 1)
                        split_lo(g + 1 + SLOTS, pair, n)
                        dve.wait_ge(gate_ready, m + (DK + 1))
                        dve.wait_ge(w_used, g + 2 + n * pair)
                        vec.tensor_tensor(up_t[i][:, :], banks[(o + 1) % BANKS][:, :], gate_t[i][:, :],
                                          ALU.mult).then_inc(out_read, 1)
                        dve.wait_ge(out_read, o + 2 + n * pair)
                        vec.tensor_tensor(up_t[i][:, :], up_t[i][:, :], tile(mix_b, m), ALU.add).then_inc(mixed, 1)
                        dve.wait_ge(m_hi_ready, m + 1)
                        lo(tile(m_lo, m), up_t[i][:, :], tile(m_hi, m)).then_inc(m_lo_ready, 1)

                with dve.Fori(0, DK // 2 - 1) as pair:
                    mix(pair)
                mix(DK // 2 - 1)
                for m in range(DK):
                    split_lo(G_OUT + m + SLOTS)
                    dve.wait_ge(w_used, G_OUT + m + 1)
                    residual(NORM_FFN2, m, O_OUT + m, 1.0)
                    dve.wait_ge(out_read, O_OUT + m + 1)
                    new_h_lo(NORM_FFN2, m)

            mean(NORM_FINAL)
            dve.wait_ge(rinv_ready, NORM_FINAL + 1)
            dve.wait_ge(y_rows_ready, DK)
            for t in range(0, TB, 2):
                vec.tensor_scalar(y_rows[:, t, :], y_rows[:, t, :], rinv[:, t:t + 1], None,
                                  ALU.mult).then_inc(scaled_dve, 1)

        @block.gpsimd
        def _(pool):
            nc.gpsimd.memset(ident[:, :], 0.0).then_inc(ident_ready, 1)
            pool.wait_ge(ident_ready, 1)
            nc.gpsimd.affine_select(out=ident[:, :], in_=ident[:, :], compare_op=ALU.not_equal, fill=1.0, base=0,
                                    pattern=[[-1, P]], channel_multiplier=1).then_inc(ident_ready, 1)
            nc.gpsimd.memset(ones[:, :], 1.0).then_inc(fills_ready, 1)
            nc.gpsimd.memset(half[:, :], -0.5).then_inc(fills_ready, 1)
            nc.gpsimd.memset(bias_row[:, :], NEG).then_inc(fills_ready, 1)
            pool.wait_ge(fills_ready, 3)
            for n in range(4):
                for m in range(1, DK):
                    pool.wait_ge(sq_ready, DK * n + m + 1)
                    if m > 1:
                        pool.wait_ge(sum_added, (DK - 1) * n + m - 1)
                    nc.gpsimd.tensor_tensor(ssum[:, :], ssum[:, :], sq[:, m % 2, :], ALU.add).then_inc(sum_added, 1)
                pool.wait_ge(var_ready, n + 1)
                nc.gpsimd.tensor_tensor(rinv[:, :], var[:, :], half[:, :], ALU.pow).then_inc(rinv_ready, 1)
                if n == NORM_MIX:
                    pool.wait_ge(rinv_ready, n + 1)
                    nc.gpsimd.memset(kp_hi[:, :, :].bitcast(F32), 0.0).then_inc(zeros_ready, 1)
                    nc.gpsimd.memset(kp_lo[:, :, :].bitcast(F32), 0.0).then_inc(zeros_ready, 1)

        @block.tensor
        def _(pe):
            def passes(out_ap, pairs, lo_ready=None, first=True, last=True):
                for i, (w, x_) in enumerate(pairs):
                    nc.tensor.matmul(out_ap, w[0], x_[0], start=first and i == 0, stop=False)
                    nc.tensor.matmul(out_ap, w[0], x_[1], start=False, stop=False)
                if lo_ready is not None:
                    pe.wait_ge(*lo_ready)
                for i, (w, x_) in enumerate(pairs):
                    mm = nc.tensor.matmul(out_ap, w[1], x_[0], start=False, stop=last and i == len(pairs) - 1)
                return mm

            def granule(g, out_ap, x_parts, first=True, last=True, it=0, n=0, tiles=None, x_ready_at=None, done=True,
                        by_tile=False):
                s = g % SLOTS
                tiles = tiles if tiles is not None else range(granule_tiles(g))
                pe.wait_ge(w_hi_ready, g + 1 + n * it)
                for i, k in enumerate(tiles):
                    if x_ready_at:
                        x_ready_at(k)
                    xh, xl = x_parts(k)
                    nc.tensor.matmul(out_ap, w_hi[:, s, k, :], xh, start=first and i == 0, stop=False)
                    mm = nc.tensor.matmul(out_ap, w_hi[:, s, k, :], xl, start=False, stop=False)
                    if by_tile:
                        if i == 0:
                            pe.wait_ge(w_lo_ready, g + 1 + n * it)
                        mm = nc.tensor.matmul(out_ap, w_lo[:, s, k, :], xh, start=False,
                                              stop=last and i == len(tiles) - 1)
                if not by_tile:
                    pe.wait_ge(w_lo_ready, g + 1 + n * it)
                for i, k in enumerate(() if by_tile else tiles):
                    mm = nc.tensor.matmul(out_ap, w_lo[:, s, k, :], x_parts(k)[0], start=False,
                                          stop=last and i == len(tiles) - 1)
                if done:
                    mm.then_inc(w_used, 1)

            def h_parts(k):
                return tile(h_hi, k), tile(h_lo, k)

            def h_ready(n):
                def wait(k):
                    pe.wait_ge(h_hi_ready, DK * n + k + 1)
                    pe.wait_ge(h_lo_ready, DK * n + k + 1)
                return wait

            def sum_squares(n):
                pe.wait_ge(sum_added, (DK - 1) * (n + 1))
                if n == NORM_FFN1:
                    pe.wait_ge(x_ready, DK)
                for t in range(TB):
                    mm = nc.tensor.matmul(banks[B_SUM][:, 2 * t:2 * t + 2], ssum[:, t * P:(t + 1) * P], ones[:, 0:2],
                                          start=True, stop=True)
                mm.then_inc(sum_done, 1)

            def spread_factors(n):
                pe.wait_ge(diag_ready, n + 1)
                nc.tensor.matmul(banks[B_RSTD][:, :], ones[:, :], gb_t[:, :], start=True, stop=True).then_inc(rstd_done, 1)

            def x_tile(m):
                if m % 2 == 0:
                    pe.wait_ge(x_landed[m // 2], 16)
                if m >= X_BANKS:
                    pe.wait_ge(x_ready, m - X_BANKS + 1)
                for t in range(TB):
                    mm = nc.tensor.transpose(banks[x_bank(m)][:, t * P:(t + 1) * P],
                                             x_rows[:, t, m * P:(m + 1) * P], ident[:, :])
                mm.then_inc(turned, 1)

            pe.wait_ge(ident_ready, 2)
            pe.wait_ge(gain_landed, 16)
            nc.tensor.transpose(banks[0][:, 0:DK], gain_rows[:, :], ident[0:DK, 0:DK]).then_inc(gain_turned, 1)
            for m in range(DK):
                x_tile(m)
            def other_constants():
                pe.wait_ge(rows_landed, 16 * 4)
                nc.tensor.transpose(banks[6][:, 0:ROWS - DK], rows[0:ROWS - DK, 0:P], ident[0:ROWS - DK, 0:ROWS - DK]
                                    ).then_inc(consts_turned, 1)
                pe.wait_ge(buckets_landed, 32)
                nc.tensor.matmul(banks[7][0:N_HEADS, 0:NREL + 1], table_b[:, :], onehot[:, :], start=True,
                                 stop=True).then_inc(bias_done, 1)

            def ffn_up(r, it, first=False, n=SLOTS):
                nrm = NORM_FFN1 if r == 0 else NORM_FFN2
                for j in range(SLOTS):
                    g, o = G_UP[r] + j, O_UP[r] + j
                    if not first or o - 3 > 0:
                        pe.wait_ge(out_read, o - 3 + n * it)
                    if first and r == 0 and j >= 2:
                        pe.wait_ge(x_ready, DK)
                    granule(g, banks[o % BANKS][:, :], h_parts, it=it, n=n, by_tile=first and j == 0,
                            x_ready_at=h_ready(nrm) if first and j == 0 else None)
                    if first and j == 1:
                        sum_squares(nrm)
                        if r == 0:
                            other_constants()
                    if first and j == 2:
                        spread_factors(nrm)

            def a_parts(at_):
                return lambda k: (tile(a_hi, at_ + k), tile(a_lo, at_ + k))

            def turn_rows(m, odd):
                pe.wait_ge(h_hi_ready, m + (DK * NORM_FINAL + 1))
                if not isinstance(m, int) or m >= 2:
                    pe.wait_ge(y_rows_ready, m - 1)
                for t in range(TB):
                    mm = nc.tensor.transpose(banks[6 + odd][:, t * P:(t + 1) * P],
                                             gate_t[odd][:, t * P:(t + 1) * P], ident[:, :])
                mm.then_inc(y_turned, 1)

            def ffn_down(r, it, first=False, n=2 * SLOTS):
                for c in range(2):
                    o = O_DOWN[r] + c
                    pe.wait_ge(out_read, o - 1 + 2 * it)
                    for j in range(SLOTS):
                        g = G_DOWN[r] + SLOTS * c + j

                        def a_ready(k, at_=DOWN_AT[j]):
                            if k == 0 or at_ + k >= FK - 2:
                                need = FK * r + (at_ + k + 1 if at_ + k >= FK - 2 else FK - 2)
                                pe.wait_ge(a_hi_ready, need)
                                pe.wait_ge(a_lo_ready, need)

                        granule(g, banks[o % BANKS][:, :], a_parts(DOWN_AT[j]), first=j == 0, last=j == SLOTS - 1,
                                it=it, n=n, x_ready_at=a_ready if c == 0 and j in (0, SLOTS - 1) else None)
                        if r == 1 and j == 1 and not (first and c == 0):
                            turn_rows(2 * it + c - 1, 1 - c)

            for r in range(2):
                ffn_up(r, 0, first=True)
                with pe.Fori(1, FK // 2) as it:
                    ffn_up(r, it)
                ffn_down(r, 0, first=True)
                with pe.Fori(1, DK // 2) as it:
                    ffn_down(r, it)
                if r == 1:
                    break

                for step in steps:
                    kind = step[0]
                    if kind == "f":
                        grp = step[1]
                        o = O_F + grp
                        pe.wait_ge(out_read, o - 1 if grp < 2 else o - 3)
                        granule(G_F + grp, banks[o % BANKS][:, :], h_parts, by_tile=grp == 0,
                                x_ready_at=h_ready(NORM_MIX) if grp == 0 else None)
                        if grp == 0:
                            sum_squares(NORM_MIX)
                        if grp == 1:
                            spread_factors(NORM_MIX)
                    elif kind in ("k", "v", "q"):
                        i = {"k": 0, "v": 1, "q": 2}[kind] + (step[1] if kind == "q" else 0)
                        o = O_K + i
                        pe.wait_ge(out_read, o - 3)
                        granule(G_K + i, banks[o % BANKS][:, :], h_parts)
                    elif kind == "turn_v":
                        pe.wait_ge(out_read, O_V + 1)
                        pe.wait_ge(ab_lo_ready, 2 * N_FGROUPS)
                        for t in range(TB):
                            mm = nc.tensor.transpose(banks[B_CH][:, t * P:(t + 1) * P], ua_t[:, t * P:(t + 1) * P],
                                                     ident[:, :])
                        mm.then_inc(v_turned, 1)
                    elif kind == "channels":
                        grp = step[1]
                        pe.wait_ge(proj_lo_ready, grp + 1)
                        if grp == 0:
                            pe.wait_ge(tab_lo_ready, 1)
                        else:
                            pe.wait_ge(ab_lo_ready, 2 * grp)
                        ch = slice(CH_AT, CH_AT + 2 * FG_DIM)
                        for t in range(TB):
                            tok = slice(t * P, (t + 1) * P)
                            o_ap = banks[B_CH + t // 2][:, (t % 2) * 2 * FG_DIM:(t % 2 + 1) * 2 * FG_DIM]
                            mm = passes(o_ap, [((fy_hi[:, grp, tok], fy_lo[:, grp, tok]),
                                                (tab_hi[:, ch], tab_lo[:, ch]))])
                            if t % 2:
                                mm.then_inc(ab_done, 1)
                    elif kind == "positions":
                        grp = step[1]
                        pe.wait_ge(ab_lo_ready, 2 * grp + 2)
                        if grp:
                            pe.wait_ge(y_ready, 2 * grp)
                        for odd in range(2):
                            pairs = []
                            for t in range(TB):
                                c0 = slice(odd * FG_DIM, (odd + 1) * FG_DIM)
                                k0 = (2 * t + odd) * NPOS
                                pairs.append(((ab_hi[:, t, c0], ab_lo[:, t, c0]),
                                              (tab_hi[:, k0:k0 + NPOS], tab_lo[:, k0:k0 + NPOS])))
                            passes(banks[B_POS + odd][:, 0:NPOS], pairs).then_inc(odd_done if odd else even_done, 1)
                    elif kind == "scores":
                        u, c = step[1:]
                        nb, kv = u // N_KV, u % N_KV
                        blocks, _ = window(nb)
                        keys = slice(blocks[0] * BLK, (blocks[-1] + 1) * BLK)
                        q = slice(nb * BLK, (nb + 1) * BLK)
                        if u == 0:
                            pe.wait_ge(proj_lo_ready, N_FGROUPS + 2 + c)
                            pe.wait_ge(v_lo_ready, 1)
                        if GQ * u + c >= 2:
                            pe.wait_ge(s_read, GQ * u + c - 1)
                        passes(banks[B_S + c % 2][:, 0:len(blocks) * BLK],
                               [((qo_hi[:, c, q], qo_lo[:, c, q]), (kp_hi[:, kv, keys], kp_lo[:, kv, keys]))]
                               ).then_inc(s_done, 1)
                    elif kind == "turn":
                        u, b = step[1:]
                        t = turn_index(u, b)
                        pe.wait_ge(probs_ready, u + 1)
                        if t >= 2:
                            pe.wait_ge(pt_lo_ready, t - 1)
                        elif t == 0:
                            pe.wait_ge(out_read, O_Q + 1)
                            pe.wait_ge(y_ready, 2 * N_FGROUPS)
                        for c in range(GQ):
                            mm = nc.tensor.transpose(banks[B_PT[t % 2]][:, c * BLK:(c + 1) * BLK],
                                                     s_t[u % 2][:, c, b * BLK:(b + 1) * BLK], ident[:, :])
                        mm.then_inc(pt_done, 1)
                    elif kind == "values":
                        u, b = step[1:]
                        t = turn_index(u, b)
                        blocks, _ = window(u // N_KV)
                        blk = blocks[b]
                        if t == 0:
                            pe.wait_ge(out_read, O_Q + 2)
                        if b == 0 and u >= 2:
                            pe.wait_ge(o_lo_ready, u - 1)
                        o_bank = banks[B_O[u % 2]][:, :]
                        pe.wait_ge(pt_hi_ready, t + 1)
                        nc.tensor.matmul(o_bank, v_hi[:, blk, :], pt_hi[:, t % 2, :], start=b == 0, stop=False)
                        nc.tensor.matmul(o_bank, v_lo[:, blk, :], pt_hi[:, t % 2, :], start=False, stop=False)
                        pe.wait_ge(pt_lo_ready, t + 1)
                        nc.tensor.matmul(o_bank, v_hi[:, blk, :], pt_lo[:, t % 2, :], start=False,
                                         stop=b == len(blocks) - 1).then_inc(pt_used, 1)
                    elif kind == "gate_b":
                        pair, i, quarter = step[1:]
                        if quarter == 0:
                            pe.wait_ge(out_read, O_B + SLOTS * pair + i - 1)
                        granule(G_B + SLOTS * pair + i, banks[i][:, :], h_parts, first=quarter == 0, last=quarter == 3,
                                tiles=range(2 * quarter, 2 * quarter + 2), done=quarter == 3)
                    elif kind == "branch_b":
                        pair, i, half_ = step[1:]
                        if half_ == 0:
                            pe.wait_ge(out_read, O_B + SLOTS * pair + 2 + i - 1)
                            pe.wait_ge(y_lo_ready, N_FGROUPS)
                        granule(G_B + SLOTS * pair + 2 + i, banks[i][:, :],
                                lambda k: (fy_hi[:, k, :], fy_lo[:, k, :]), first=half_ == 0, last=half_ == 1,
                                tiles=range(2 * half_, 2 * half_ + 2), done=half_ == 1)

                with pe.Fori(0, DK // 2) as pair:
                    pe.wait_ge(pt_lo_ready, turn_index(TB * N_KV, 0))
                    for j in range(SLOTS):
                        if j == 1:
                            pe.wait_ge(o_lo_ready, TB * N_KV)
                        o = O_A + j
                        pe.wait_ge(out_read, o - 3 + SLOTS * pair)
                        granule(G_A + j, banks[o % BANKS][:, :],
                                (lambda k: (qo_hi[:, k, :], qo_lo[:, k, :])) if j % 2 else h_parts,
                                it=pair, n=SLOTS)

                def mixed_ready(k):
                    if k == 0 or k == DK - 1:
                        need = DK - 1 if k == 0 else DK
                        pe.wait_ge(m_hi_ready, need)
                        pe.wait_ge(m_lo_ready, need)

                for j in range(DK):
                    o = O_OUT + j
                    pe.wait_ge(out_read, o - 3)
                    granule(G_OUT + j, banks[o % BANKS][:, :], lambda k: (tile(m_hi, k), tile(m_lo, k)),
                            x_ready_at=mixed_ready if j == 0 else None, by_tile=j == 0)

            turn_rows(DK - 1, 1)
            sum_squares(NORM_FINAL)


INPUTS = ["x", "g_ffn1", "w_up1", "w_down1", "g_mix", "w_in", "b_gate", "sink", "rel_bias", "w_branch_a",
          "w_branch_b", "w_out", "g_ffn2", "w_up2", "w_down2", "g_final"]


def kernel(**inputs):
    import concourse.bacc as bacc
    from concourse.bass_utils import run_bass_kernel_spmd

    nc = bacc.Bacc("TRN2", target_bir_lowering=False, num_devices=1)
    arrays, io = {}, {}
    host = {name: np.ascontiguousarray(inputs[name]) for name in INPUTS}
    host.update(shape_constants())
    for name, a in host.items():
        arrays[f"in_{name}_dram"] = a
        io[name] = nc.dram_tensor(f"in_{name}_dram", a.shape, mybir.dt.from_np(a.dtype), kind="ExternalInput").ap()
    io["out"] = nc.dram_tensor("out_dram", (1, SEQ, D_MODEL), F32, kind="ExternalOutput").ap()
    build(nc, io)
    r = run_bass_kernel_spmd(nc, [arrays], core_ids=[0])
    return r.results[0]["out_dram"]
```

```python
from contextlib import ExitStack

import numpy as np

import concourse.bass as bass
from concourse import mybir

F32 = mybir.dt.float32
F32R = mybir.dt.float32r
ACT = mybir.ActivationFunctionType
ALU = mybir.AluOpType

P = 128
SEQ, D_MODEL, D_FF = 512, 1024, 2816
N_HEADS, N_KV, HD = 8, 2, 64
GQ = N_HEADS // N_KV
BLK = WINDOW = 128
N_BUCKETS, MAX_DIST = 32, 128
N_FGROUPS, FG_DIM = 4, 128
Q_WIDTH, KV_WIDTH, F_WIDTH = N_HEADS * HD, N_KV * HD, N_FGROUPS * FG_DIM
EPS, NEG = 1e-6, -1e30

DK = D_MODEL // P
FK = D_FF // P
TB = SEQ // P
SLOTS = 4
BANKS = 4
DOWN_PARTS = [6, 6, 5, 5]
DOWN_AT = [sum(DOWN_PARTS[:i]) for i in range(len(DOWN_PARTS))]
assert sum(DOWN_PARTS) == FK and len(DOWN_PARTS) == SLOTS

G_UP = [0, None]
G_DOWN = [2 * FK, None]
G_F = G_DOWN[0] + SLOTS * DK
G_K = G_F + N_FGROUPS
G_V, G_Q = G_K + 1, G_K + 2
G_B = G_Q + GQ
G_A = G_B + 2 * DK
G_OUT = G_A + 2 * DK
G_UP[1] = G_OUT + DK
G_DOWN[1] = G_UP[1] + 2 * FK
G_END = G_DOWN[1] + SLOTS * DK
O_UP = [0, None]
O_DOWN = [2 * FK, None]
O_F = O_DOWN[0] + DK
O_K = O_F + N_FGROUPS
O_V, O_Q = O_K + 1, O_K + 2
O_B = O_Q + GQ
O_A = O_B + 2 * DK
O_OUT = O_A + 2 * DK
O_UP[1] = O_OUT + DK
O_DOWN[1] = O_UP[1] + 2 * FK
NORM_FFN1, NORM_MIX, NORM_FFN2, NORM_FINAL = range(4)
B_SUM, B_RSTD = 4, 5
B_CH, B_POS = 4, 6
B_S = 4
B_PT, B_O = [2, 6], 3
B_B = [7, 0, 1]
HALF = SEQ // 2
NPOS = SEQ // 2 + 2
CH_AT = TB * 2 * NPOS
TABLE = CH_AT + 2 * FG_DIM
X_BANKS = 6
X_ORDER = [("h", 0), ("w", 0), ("h", 1), ("h", 2), ("x", 0), ("h", 3), ("h", 4), ("x", 1), ("h", 5),
           ("h", 6), ("s", 0), ("h", 7), ("x", 2), ("w", 1), ("x", 3), ("x", 4), ("s", 1), ("s", 2),
           ("s", 3), ("x", 5), ("x", 6), ("x", 7), ("w", 2), ("s", 4), ("s", 5), ("s", 6), ("s", 7),
           ("w", 3)]
NREL = 2 * WINDOW + 1
ROWS = 4 * DK + 2 * DK


def t5_buckets():
    rel = np.arange(-WINDOW, WINDOW + 1)
    half = N_BUCKETS // 2
    max_exact = half // 2
    n = np.abs(rel)
    n_safe = np.maximum(n, 1).astype(np.float32)
    large = max_exact + (np.log(n_safe / max_exact) / np.log(MAX_DIST / max_exact)
                         * (half - max_exact)).astype(np.int32)
    large = np.minimum(large, half - 1)
    return (rel > 0).astype(np.int32) * half + np.where(n < max_exact, n, large)


def shape_constants():
    s, k = np.arange(SEQ)[:, None], np.arange(NPOS)[None, :]
    turn = 2 * np.pi * ((s * k) % SEQ) / SEQ
    scale = 1.0 / np.sqrt(SEQ * FG_DIM)
    pos = np.concatenate([np.cos(turn) * scale, -np.sin(turn) * scale], axis=1)
    pos = pos.reshape(TB, P, 2 * NPOS).transpose(1, 0, 2).reshape(P, CH_AT)
    c = np.arange(FG_DIM)
    turn = 2 * np.pi * ((c[:, None] * c[None, :]) % FG_DIM) / FG_DIM
    tables = np.concatenate([pos, np.cos(turn), np.sin(turn)], axis=1).astype(np.float32)
    onehot = np.zeros((N_BUCKETS, NREL + 1), np.float32)
    onehot[t5_buckets(), np.arange(NREL)] = 1.0
    return {"tables": tables, "onehot": onehot}


def window(nb):
    blocks = [j for j in (nb - 1, nb, nb + 1) if 0 <= j < TB]
    return blocks, blocks[0] - (nb - 1)


MIXER = """
    f 0; f 1; f 2; f 3; channels 0; k; v; positions 0; channels 1; q 0; positions 1; channels 2; q 1;
    positions 2; channels 3; q 2; turn_v; q 3; positions 3;
    scores 0 0; scores 0 1; gate_b 0 0 0; gate_b 0 0 1; scores 0 2; scores 0 3; max 0; gate_b 0 0 2; exp 0;
    scores 1 0; normalize 0; gate_b 0 0 3; gate_b 0 1 0; scores 1 1; turn 0 0; turn 0 1; scores 1 2;
    gate_b 0 1 1; values 0 0; scores 1 3; max 1; values 0 1; exp 1; normalize 1; gate_b 0 1 2; gate_b 0 1 3;
    branch_b 0 0 0; sigmoid 0;
    scores 2 0; scores 2 1; turn 1 0; branch_b 0 0 1; turn 1 1; branch_b 0 1 0; values 1 0; values 1 1;
    scores 2 2; scores 2 3; max 2; take_b 0 0; exp 2; normalize 2; branch_b 0 1 1; gate_b 1 0 0; gate_b 1 0 1;
    take_b 0 1; gate_b 1 0 2; gate_b 1 0 3; turn 2 0; turn 2 1;
    scores 3 0; scores 3 1; gate_b 1 1 0; values 2 0; turn 2 2; values 2 1; scores 3 2; scores 3 3; max 3;
    exp 3; normalize 3; gate_b 1 1 1; gate_b 1 1 2; gate_b 1 1 3; values 2 2; sigmoid 1;
    scores 4 0; branch_b 1 0 0; turn 3 0; turn 3 1; scores 4 1; branch_b 1 0 1; values 3 0; turn 3 2;
    values 3 1; scores 4 2; scores 4 3; max 4; exp 4; take_b 1 0; branch_b 1 1 0; normalize 4; values 3 2;
    branch_b 1 1 1; gate_b 2 0 0;
    scores 5 0; scores 5 1; take_b 1 1; gate_b 2 0 1; turn 4 0; turn 4 1; gate_b 2 0 2; gate_b 2 0 3;
    values 4 0; values 4 1; turn 4 2; scores 5 2; scores 5 3; max 5; exp 5; normalize 5; gate_b 2 1 0;
    values 4 2; gate_b 2 1 1; gate_b 2 1 2; gate_b 2 1 3; branch_b 2 0 0; turn 5 0; turn 5 1;
    scores 6 0; scores 6 1; values 5 0; turn 5 2; values 5 1; scores 6 2; scores 6 3; max 6; exp 6;
    branch_b 2 0 1; values 5 2; normalize 6; branch_b 2 1 0; branch_b 2 1 1; sigmoid 2; take_b 2 0; take_b 2 1;
    gate_b 3 0 0; gate_b 3 0 1; turn 6 0;
    scores 7 0; turn 6 1; gate_b 3 0 2; scores 7 1; values 6 0; scores 7 2; scores 7 3; values 6 1; max 7;
    exp 7; normalize 7; gate_b 3 0 3; gate_b 3 1 0; gate_b 3 1 1; gate_b 3 1 2; gate_b 3 1 3; turn 7 0;
    turn 7 1; branch_b 3 0 0; branch_b 3 0 1; values 7 0; branch_b 3 1 0; values 7 1; branch_b 3 1 1;
    sigmoid 3; take_b 3 0; take_b 3 1;
"""


def mixer_schedule():
    words = [step.split() for step in MIXER.replace("\n", " ").split(";") if step.strip()]
    return [(kind, *map(int, numbers)) for kind, *numbers in words]


def granule_tiles(g):
    for down in G_DOWN:
        if down <= g < down + SLOTS * DK:
            return DOWN_PARTS[(g - down) % SLOTS]
    if G_B <= g < G_A and (g - G_B) % SLOTS >= 2 or G_A <= g < G_OUT and (g - G_A) % 2:
        return GQ
    return DK


def turn_index(u, b):
    return sum(len(window(v // N_KV)[0]) for v in range(u)) + b


def build(nc, io):
    x, out = io["x"], io["out"]
    w_up = [io["w_up1"][0].rearrange("(k p) n -> p k n", p=P), io["w_up2"][0].rearrange("(k p) n -> p k n", p=P)]
    w_down = [io["w_down1"][0].rearrange("(k p) n -> p k n", p=P), io["w_down2"][0].rearrange("(k p) n -> p k n", p=P)]
    w_in = io["w_in"][0].rearrange("(k p) n -> p k n", p=P)
    w_a = io["w_branch_a"][0]
    w_b = io["w_branch_b"][0].rearrange("(k p) n -> p k n", p=P)
    w_out = io["w_out"][0].rearrange("(k p) n -> p k n", p=P)
    bias_rows = nc.dram_tensor("bias_rows", [N_HEADS, P, SEQ], F32, kind="Internal").ap()
    steps = mixer_schedule()

    with ExitStack() as ctx:
        base = 16512
        at = [base]

        def place(name, shape, dt, offset=None):
            here = at[0] if offset is None else offset
            size = int(np.prod(shape[1:])) * 4
            t = nc.alloc_sbuf_tensor_at(name, shape, dt, offset=here)
            if offset is None:
                at[0] = here + (size + 31) // 32 * 32
            return t, here, (size + 31) // 32 * 32

        xT, _, _ = place("xT", [P, DK * SEQ], F32)
        h_hi, h_at, _ = place("h_hi", [P, DK * SEQ], F32R)
        h_lo, _, _ = place("h_lo", [P, DK * SEQ], F32R)
        raw, _, _ = place("raw", [P, SLOTS, DK, P], F32)
        w_hi, _, _ = place("w_hi", [P, SLOTS, DK, P], F32R)
        w_lo, _, _ = place("w_lo", [P, SLOTS, DK, P], F32R)
        rstd, _, _ = place("rstd", [P, SEQ], F32)
        ident, _, _ = place("ident", [P, P], F32)
        ones, _, _ = place("ones", [P, P], F32)
        ssum, ssum_at, _ = place("ssum", [P, SEQ], F32)
        sq, _, _ = place("sq", [P, 2, SEQ], F32)
        ga_t, _, _ = place("ga_t", [P, SEQ], F32)
        gb_t, _, _ = place("gb_t", [P, SEQ], F32)
        ua_t, ua_at, _ = place("ua_t", [P, SEQ], F32)
        ub_t, _, _ = place("ub_t", [P, SEQ], F32)
        bias_row, br_at, _ = place("bias_row", [N_HEADS, SEQ], F32)
        assert br_at + SEQ * 4 == ua_at + 3 * SEQ * 4
        gate_t, up_t = [ga_t, gb_t], [ua_t, ub_t]
        s_a, _, _ = place("s_a", [P, GQ, 3 * BLK], F32, ssum_at)
        s_b, _, _ = place("s_b", [P, GQ, 3 * BLK], F32, ua_at)
        s_t = [s_a, s_b]
        even_t, _, _ = place("even_t", [P, NPOS], F32)
        y_t, _, _ = place("y_t", [P, SEQ], F32)
        consts, _, _ = place("consts", [P, ROWS], F32)
        rows = y_t
        warm, _, _ = place("warm", [P, 2], F32)
        sink, _, _ = place("sink", [P, N_HEADS], F32)
        half, _, _ = place("half", [P, TB], F32)
        var, _, _ = place("var", [P, TB], F32)
        rinv, _, _ = place("rinv", [P, TB], F32)
        mx, _, _ = place("mx", [P, 2, GQ], F32)
        negm, _, _ = place("negm", [P, 2, GQ], F32)
        sdiff, _, _ = place("sdiff", [P, 2, GQ], F32)
        psumr, _, _ = place("psumr", [P, 2, GQ], F32)
        esink, _, _ = place("esink", [P, 2, GQ], F32)
        den, _, _ = place("den", [P, 2, GQ], F32)
        rden, _, _ = place("rden", [P, 2, GQ], F32)
        a_hi, act_at, a_size = place("a_hi", [P, FK * SEQ], F32R)
        a_lo, _, _ = place("a_lo", [P, FK * SEQ], F32R)
        assert at[0] <= nc.sbuf_usable_end, (at[0], nc.sbuf_usable_end)
        act_end = at[0]
        x_rows, _, xr_size = place("x_rows", [P, TB, D_MODEL], F32, act_at)
        gain_rows, gr_at, gr_size = place("gain_rows", [DK, P], F32, act_at + xr_size)
        table_b, tb_at, tb_size = place("table_b", [N_BUCKETS, N_HEADS], F32, gr_at + gr_size)
        onehot, _, _ = place("onehot", [N_BUCKETS, NREL + 1], F32, tb_at + tb_size)
        here = [act_at]

        def reuse(name, shape, dt):
            t, where, size = place(name, shape, dt, here[0])
            here[0] += size
            assert here[0] <= act_end
            return t, where

        kp_hi, _ = reuse("kp_hi", [P, N_KV, SEQ], F32R)
        kp_lo, _ = reuse("kp_lo", [P, N_KV, SEQ], F32R)
        v_hi, _ = reuse("v_hi", [P, TB, P], F32R)
        v_lo, _ = reuse("v_lo", [P, TB, P], F32R)
        bias, bias_at = reuse("bias", [P, N_HEADS, 3 * BLK], F32)
        ab_hi, ab_at = reuse("ab_hi", [P, TB, 2 * FG_DIM], F32R)
        ab_lo, _ = reuse("ab_lo", [P, TB, 2 * FG_DIM], F32R)
        assert here[0] - act_at == 2 * DK * SEQ * 4
        tab_hi, tab_at = reuse("tab_hi", [P, TABLE], F32R)
        tab_lo, _ = reuse("tab_lo", [P, TABLE], F32R)
        qo_hi, _ = reuse("qo_hi", [P, GQ, SEQ], F32R)
        qo_lo, _ = reuse("qo_lo", [P, GQ, SEQ], F32R)
        fy_hi, _ = reuse("fy_hi", [P, N_FGROUPS, SEQ], F32R)
        fy_lo, _ = reuse("fy_lo", [P, N_FGROUPS, SEQ], F32R)
        tab_raw, _, _ = place("tab_raw", [P, TABLE], F32, bias_at)
        pt_hi, pt_at, pt_size = place("pt_hi", [P, 2, GQ * BLK], F32R, ab_at)
        pt_lo, _, _ = place("pt_lo", [P, 2, GQ * BLK], F32R, ab_at + pt_size)
        mix_b, _, _ = place("mix_b", [P, DK * SEQ], F32, tab_at)
        m_hi, _, m_size = place("m_hi", [P, DK * SEQ], F32R, act_at)
        m_lo, _, _ = place("m_lo", [P, DK * SEQ], F32R, act_at + m_size)
        y_rows, _, _ = place("y_rows", [P, TB, D_MODEL], F32, h_at)

        banks = [ctx.enter_context(nc.psum_tensor(f"bank{i}", [P, SEQ], F32)) for i in range(8)]

        def sem(name):
            return ctx.enter_context(nc.semaphore(name))

        x_landed = [sem(f"x_landed{i}") for i in range(4)]
        gain_landed = sem("gain_landed")
        rows_landed, buckets_landed, sink_landed = sem("rows_landed"), sem("buckets_landed"), sem("sink_landed")
        raw_landed = [sem(f"raw_landed{i}") for i in range(SLOTS)]
        q_second, a_second = [sem(f"q_second{i}") for i in range(GQ)], [sem(f"a_second{i}") for i in range(2)]
        bias_stored, bias_landed, tables_landed = sem("bias_stored"), sem("bias_landed"), sem("tables_landed")
        out_stored = sem("out_stored")
        ident_ready, fills_ready = sem("ident_ready"), sem("fills_ready")
        sum_added, rinv_ready, zeros_ready = sem("sum_added"), sem("rinv_ready"), sem("zeros_ready")
        w_hi_ready, h_hi_ready, sq_ready = sem("w_hi_ready"), sem("h_hi_ready"), sem("sq_ready")
        silu_ready, a_hi_ready, gate_ready = sem("silu_ready"), sem("a_hi_ready"), sem("gate_ready")
        proj_hi_ready, tab_hi_ready, exp_ready = sem("proj_hi_ready"), sem("tab_hi_ready"), sem("exp_ready")
        pt_hi_ready, o_hi_ready, ab_hi_ready = sem("pt_hi_ready"), sem("o_hi_ready"), sem("ab_hi_ready")
        even_copied, y_hi_ready, m_hi_ready = sem("even_copied"), sem("y_hi_ready"), sem("m_hi_ready")
        last_squared, y_rows_ready, scaled_act = sem("last_squared"), sem("y_rows_ready"), sem("scaled_act")
        w_lo_ready, h_lo_ready, x_ready = sem("w_lo_ready"), sem("h_lo_ready"), sem("x_ready")
        out_read, product_ready, a_lo_ready = sem("out_read"), sem("product_ready"), sem("a_lo_ready")
        gain_ready, consts_ready, row_ready = sem("gain_ready"), sem("consts_ready"), sem("row_ready")
        var_ready, diag_ready, rstd_ready = sem("var_ready"), sem("diag_ready"), sem("rstd_ready")
        proj_lo_ready, v_lo_ready, tab_lo_ready = sem("proj_lo_ready"), sem("v_lo_ready"), sem("tab_lo_ready")
        v_hi_ready = sem("v_hi_ready")
        s_read, max_ready, den_ready, probs_ready = sem("s_read"), sem("max_ready"), sem("den_ready"), sem("probs_ready")
        pt_lo_ready, o_lo_ready, ab_lo_ready = sem("pt_lo_ready"), sem("o_lo_ready"), sem("ab_lo_ready")
        y_ready, y_lo_ready = sem("y_ready"), sem("y_lo_ready")
        last_updated, last_scaled = sem("last_updated"), sem("last_scaled")
        mixed, m_lo_ready, scaled_dve = sem("mixed"), sem("m_lo_ready"), sem("scaled_dve")
        w_used, turned, bias_done = sem("w_used"), sem("turned"), sem("bias_done")
        gain_turned, consts_turned = sem("gain_turned"), sem("consts_turned")
        sum_done, rstd_done, v_turned = sem("sum_done"), sem("rstd_done"), sem("v_turned")
        s_done, pt_done, o_done = sem("s_done"), sem("pt_done"), sem("o_done")
        pt_used, last_done = sem("pt_used"), sem("last_done")
        ab_done, even_done, odd_done, y_turned = sem("ab_done"), sem("even_done"), sem("odd_done"), sem("y_turned")

        block = ctx.enter_context(nc.Block())

        def tile(t, m):
            if isinstance(m, int):
                return t[:, m * SEQ:(m + 1) * SEQ]
            return t[:, bass.ds(m * SEQ, SEQ)]

        def x_bank(m):
            return 8 - X_BANKS + m % X_BANKS

        def last_bank(h):
            return (O_DOWN[1] + DK - 1 + h) % BANKS

        def gain(n, m):
            if isinstance(m, int):
                return consts[:, n * DK + m:n * DK + m + 1]
            return consts[:, bass.ds(m + n * DK, 1)]


        @block.sync
        def _(sp):
            def load(g, dst, src, it=0, n=0):
                if g >= SLOTS or n:
                    sp.wait_ge(w_lo_ready, g - SLOTS + 1 + n * it)
                sp.dma_start(dst, src).then_inc(raw_landed[g % SLOTS], 16)

            def up(r, it, j, n=0):
                g = G_UP[r] + j
                col = it * (2 * P) + (j // 2) * P + (j % 2) * D_FF
                cols = slice(col, col + P) if isinstance(it, int) else bass.ds(sp.snap(col), P)
                load(g, raw[:, g % SLOTS, :, :], w_up[r][:, :, cols], it, n)

            def down(r, m, j, n=0):
                g = G_DOWN[r] + j
                k0, nk = DOWN_AT[j], DOWN_PARTS[j]
                load(g, raw[:, g % SLOTS, 0:nk, :], w_down[r][:, k0:k0 + nk, bass.ds(sp.snap(m * P), P)], m, n)

            xv = x[0].rearrange("(t p) d -> p t d", p=P)
            for c in range(4):
                w = D_MODEL // 4
                sp.dma_start(x_rows[:, :, c * w:(c + 1) * w], xv[:, :, c * w:(c + 1) * w]).then_inc(x_landed[c], 16)
                if c == 0:
                    up(0, 0, 0)
            for r in range(2):
                if r == 0:
                    for j in range(1, SLOTS):
                        up(0, 0, j)
                    r0 = 0
                    for name, nr in (("g_mix", DK), ("g_ffn2", DK), ("g_final", DK), ("b_gate", 2 * DK)):
                        v = io[name] if name == "g_final" else io[name][0]
                        sp.dma_start(rows[r0:r0 + nr, 0:P], v.rearrange("(r p) -> r p", p=P)).then_inc(rows_landed, 16)
                        r0 += nr
                    sp.dma_start(table_b[:, :], io["rel_bias"]).then_inc(buckets_landed, 16)
                    sp.dma_start(onehot[:, :], io["onehot"]).then_inc(buckets_landed, 16)
                    sp.dma_start(sink[:, :], io["sink"].broadcast_to([P, N_HEADS])).then_inc(sink_landed, 16)
                with sp.Fori(1 - r, FK // 2) as it:
                    for j in range(SLOTS):
                        up(r, it, j, SLOTS)
                with sp.Fori(0, DK) as m:
                    for j in range(SLOTS):
                        down(r, m, j, SLOTS)
                if r == 1:
                    break
                for c in range(N_FGROUPS):
                    g, col = G_F + c, Q_WIDTH + 2 * KV_WIDTH + c * FG_DIM
                    load(g, raw[:, g % SLOTS, :, :], w_in[:, :, col:col + P])
                for g, col in ((G_K, Q_WIDTH), (G_V, Q_WIDTH + KV_WIDTH)):
                    load(g, raw[:, g % SLOTS, :, :], w_in[:, :, col:col + P])
                q_cols = w_in[:, :, 0:Q_WIDTH].rearrange("p k (v c d) -> p k v c d", v=N_KV, c=GQ)
                for c in range(GQ):
                    g = G_Q + c
                    load(g, raw[:, g % SLOTS, :, 0:HD], q_cols[:, :, 0, c, :])
                    sp.dma_start(raw[:, g % SLOTS, :, HD:P], q_cols[:, :, 1, c, :]).then_inc(q_second[c], 16)
                gates_at = Q_WIDTH + 2 * KV_WIDTH + F_WIDTH
                for pair in range(DK // 2):
                    g0 = G_B + SLOTS * pair
                    for i in range(2):
                        col = gates_at + D_MODEL + (2 * pair + i) * P
                        load(g0 + i, raw[:, (g0 + i) % SLOTS, :, :], w_in[:, :, col:col + P])
                    for i in range(2):
                        g, col = g0 + 2 + i, (2 * pair + i) * P
                        load(g, raw[:, g % SLOTS, 0:N_FGROUPS, :], w_b[:, :, col:col + P])
                wa_v = w_a.rearrange("(v c d) n -> v d c n", v=N_KV, c=GQ)
                with sp.Fori(0, DK // 2) as pair:
                    for i in range(2):
                        g = G_A + 2 * i
                        cols = bass.ds(sp.snap(pair * (2 * P) + (gates_at + i * P)), P)
                        load(g, raw[:, g % SLOTS, :, :], w_in[:, :, cols], pair, SLOTS)
                        g = G_A + 2 * i + 1
                        cols = bass.ds(sp.snap(pair * (2 * P) + i * P), P)
                        load(g, raw[HD:P, g % SLOTS, 0:GQ, :], wa_v[1, :, :, cols], pair, SLOTS)
                        sp.dma_start(raw[0:HD, g % SLOTS, 0:GQ, :], wa_v[0, :, :, cols]).then_inc(a_second[i], 16)
                with sp.Fori(0, DK // SLOTS) as it:
                    for j in range(SLOTS):
                        g = G_OUT + j
                        load(g, raw[:, g % SLOTS, :, :], w_out[:, :, bass.ds(sp.snap(it * (SLOTS * P) + j * P), P)], it, SLOTS)
            ov = out[0].rearrange("(t p) d -> p t d", p=P)
            for h in range(2):
                for c in range(2):
                    cols = slice(c * D_MODEL // 2, (c + 1) * D_MODEL // 2)
                    sp.wait_ge(scaled_dve, 2 * h + c + 1)
                    sp.dma_start(ov[:, 2 * h, cols], y_rows[:, 2 * h, cols]).then_inc(out_stored, 16)
                    sp.wait_ge(scaled_act, 2 * h + c + 1)
                    sp.dma_start(ov[:, 2 * h + 1, cols], y_rows[:, 2 * h + 1, cols]).then_inc(out_stored, 16)
            sp.wait_ge(out_stored, 16 * 2 * TB)

        @block.scalar
        def _(act):
            def copy(dst, src, scale=1.0):
                return nc.scalar.activation(dst, src, ACT.Copy, scale=scale)

            def split_hi(g, it=0, n=0):
                s, static = g % SLOTS, isinstance(it, int)
                nk = granule_tiles(g + n * it if static else g)
                act.wait_ge(raw_landed[s], 16 * (g // SLOTS + 1) + 4 * n * it)
                if static and G_Q <= g + n * it < G_Q + GQ:
                    act.wait_ge(q_second[g + n * it - G_Q], 16)
                at_a = g - G_A if not static or n == 0 else g + n * it - G_A
                if 0 <= at_a < 2 * DK and at_a % 2:
                    turn_ = at_a // SLOTS + (0 if static else it)
                    act.wait_ge(a_second[at_a % SLOTS // 2], 16 * turn_ + 16)
                if g >= SLOTS:
                    act.wait_ge(w_used, g - SLOTS + 1 + n * it)
                copy(w_hi[:, s, 0:nk, :], raw[:, s, 0:nk, :]).then_inc(w_hi_ready, 1)

            def square_free(n, m):
                if not isinstance(m, int) or m >= 3:
                    act.wait_ge(sum_added, m + ((DK - 1) * n - 2))

            def residual(n, m, odd, first=False):
                if n < NORM_FINAL:
                    copy(tile(h_hi, m), tile(xT, m), scale=gain(n, m)).then_inc(h_hi_ready, 1)
                else:
                    copy(gate_t[odd][:, :], tile(xT, m), scale=gain(n, m)).then_inc(h_hi_ready, 1)
                square(tile(xT, m), odd, first)

            def square(src, odd, first):
                nc.scalar.activation(ssum[:, :] if first else sq[:, odd, :], src, ACT.Square).then_inc(sq_ready, 1)

            act.dma_start(gain_rows[:, :], io["g_ffn1"][0].rearrange("(r p) -> r p", p=P)).then_inc(gain_landed, 16)
            act.wait_ge(fills_ready, 1)
            nc.scalar.activation(warm[:, :], ones[:, 0:2], ACT.Silu)
            act.wait_ge(gain_ready, 1)

            def x_hi(m):
                act.wait_ge(turned, m + 1)
                copy(tile(h_hi, m), banks[x_bank(m)][:, :], scale=gain(NORM_FFN1, m)).then_inc(h_hi_ready, 1)

            def x_square(m):
                act.wait_ge(x_ready, m + 1)
                square_free(NORM_FFN1, m)
                square(tile(xT, m), m % 2, m == 0)

            for piece in X_ORDER:
                if piece[0] == "h":
                    x_hi(piece[1])
                elif piece[0] == "s":
                    x_square(piece[1])
                elif piece[0] == "w":
                    split_hi(piece[1])

            def ffn_up(r, it, n=SLOTS):
                for j in range(2):
                    g, o = G_UP[r] + 2 * j, O_UP[r] + 2 * j
                    split_hi(g + SLOTS, it, n)
                    act.wait_ge(out_read, o + 1 + n * it)
                    nc.scalar.activation(gate_t[j][:, :], gate_t[j][:, :], ACT.Silu).then_inc(silu_ready, 1)
                    split_hi(g + 1 + SLOTS, it, n)
                    act.wait_ge(product_ready, FK * r + j + 1 + 2 * it)
                    copy(tile(a_hi, 2 * it + j), up_t[j][:, :]).then_inc(a_hi_ready, 1)

            def turned_rows(m, odd):
                act.wait_ge(y_turned, m + 1)
                dst = y_rows[:, :, m * P:(m + 1) * P] if isinstance(m, int) else y_rows[:, :, bass.ds(m * P, P)]
                copy(dst, banks[6 + odd][:, :].rearrange("p (t d) -> p t d", t=TB)).then_inc(y_rows_ready, 1)

            def ffn_down(r, it, first=False, last=False, n=2 * SLOTS):
                for j in range(2):
                    g, m = G_DOWN[r] + SLOTS * j, 2 * it + j
                    ahead = not (r == 1 and last and j == 1)
                    if ahead:
                        for i in range(3):
                            split_hi(g + SLOTS + i, it, n)
                    if r == 1 and not (first and j == 0):
                        turned_rows(m - 1, 1 - j)
                    if not ahead:
                        break
                    nrm = NORM_MIX if r == 0 else NORM_FINAL
                    square_free(nrm, m)
                    act.wait_ge(out_read, O_DOWN[r] + j + 1 + 2 * it)
                    residual(nrm, m, j, first and j == 0)
                    if ahead:
                        split_hi(g + SLOTS + 3, it, n)

            for r in range(2):
                with act.Fori(0, FK // 2 - 1) as it:
                    ffn_up(r, it)
                ffn_up(r, FK // 2 - 1)
                if r == 0:
                    act.wait_ge(consts_ready, 1)
                    act.wait_ge(row_ready, 1)
                    act.dma_start(bias_rows, bias_row[:, :].unsqueeze(1).broadcast_to([N_HEADS, P, SEQ])
                                  ).then_inc(bias_stored, 16)
                ffn_down(r, 0, first=True)
                with act.Fori(1, DK // 2 - 1) as it:
                    ffn_down(r, it)
                ffn_down(r, DK // 2 - 1, last=True)
                if r == 1:
                    break

                act.dma_start(tab_raw[:, :], io["tables"]).then_inc(tables_landed, 16)
                for step in steps:
                    kind = step[0]
                    if kind == "f":
                        grp = step[1]
                        split_hi(G_F + grp + SLOTS)
                        act.wait_ge(out_read, O_F + grp + 1)
                        copy(fy_hi[:, grp, :], gate_t[grp % 2][:, :]).then_inc(proj_hi_ready, 1)
                        if grp == 1:
                            act.wait_ge(tables_landed, 16)
                            copy(tab_hi[:, :], tab_raw[:, :]).then_inc(tab_hi_ready, 1)
                    elif kind == "k":
                        split_hi(G_K + SLOTS)
                        act.wait_ge(zeros_ready, 2)
                        act.wait_ge(out_read, O_K + 1)
                        for v in range(N_KV):
                            rows_v = slice(v * HD, (v + 1) * HD)
                            last = copy(kp_hi[rows_v, v, :], ga_t[rows_v, :])
                        last.then_inc(proj_hi_ready, 1)
                        act.wait_ge(tab_lo_ready, 1)
                        act.wait_ge(bias_stored, 16)
                        diagonals = bias_rows.rearrange("h q m -> h (q m)")[:, BLK - 1:BLK - 1 + P * (SEQ - 1)]
                        diagonals = diagonals.rearrange("h (q m) -> q h m", m=SEQ - 1)[:, :, 0:3 * BLK]
                        act.dma_start(bias[:, :, :], diagonals).then_inc(bias_landed, 16)
                    elif kind == "v":
                        split_hi(G_V + SLOTS)
                    elif kind == "q":
                        c = step[1]
                        split_hi(G_Q + c + SLOTS)
                        act.wait_ge(out_read, O_Q + c + 1)
                        copy(qo_hi[:, c, :], gate_t[(c + 1) % 2][:, :]).then_inc(proj_hi_ready, 1)
                    elif kind == "turn_v":
                        act.wait_ge(v_turned, 1)
                        copy(v_hi[:, :, :], banks[B_CH][:, :]).then_inc(v_hi_ready, 1)
                    elif kind == "channels":
                        grp = step[1]
                        for i in range(2):
                            act.wait_ge(ab_done, 2 * grp + i + 1)
                            copy(ab_hi[:, 2 * i:2 * i + 2, :], banks[B_CH + i][:, :]).then_inc(ab_hi_ready, 1)
                    elif kind == "positions":
                        grp = step[1]
                        act.wait_ge(even_done, grp + 1)
                        if grp:
                            act.wait_ge(y_ready, 2 * grp)
                        copy(even_t[:, :], banks[B_POS][:, 0:NPOS]).then_inc(even_copied, 1)
                        act.wait_ge(y_ready, 2 * grp + 2)
                        copy(fy_hi[:, grp, :], y_t[:, :]).then_inc(y_hi_ready, 1)
                    elif kind == "exp":
                        u = step[1]
                        width = len(window(u // N_KV)[0]) * BLK
                        act.wait_ge(max_ready, 3 * u + 3)
                        for c in range(GQ):
                            sc = s_t[u % 2][:, c, 0:width]
                            nc.scalar.activation(sc, sc, ACT.Exp, bias=negm[:, u % 2, c:c + 1],
                                                 accum_out=psumr[:, u % 2, c:c + 1])
                        nc.scalar.activation(esink[:, u % 2, :], sdiff[:, u % 2, :], ACT.Exp).then_inc(exp_ready, 1)
                    elif kind == "turn":
                        t = turn_index(*step[1:])
                        act.wait_ge(pt_done, t + 1)
                        if t >= 2:
                            act.wait_ge(pt_used, t - 1)
                        copy(pt_hi[:, t % 2, :], banks[B_PT[t % 2]][:, :]).then_inc(pt_hi_ready, 1)
                    elif kind == "values":
                        u, b = step[1:]
                        nb, kv = u // N_KV, u % N_KV
                        if b == len(window(nb)[0]) - 1:
                            rows_v = slice(kv * HD, (kv + 1) * HD)
                            act.wait_ge(pt_used, turn_index(u, b) + 1)
                            copy(qo_hi[rows_v, :, nb * BLK:(nb + 1) * BLK],
                                 banks[B_O][rows_v, :].rearrange("p (c q) -> p c q", c=GQ)
                                 ).then_inc(o_hi_ready, 1)
                    elif kind == "gate_b" and step[3] == 3:
                        split_hi(G_B + SLOTS * step[1] + step[2] + SLOTS)
                    elif kind == "sigmoid":
                        pair = step[1]
                        for i in range(2):
                            b = 5 * DK + 2 * pair + i
                            act.wait_ge(out_read, O_B + SLOTS * pair + i + 1)
                            nc.scalar.activation(gate_t[i][:, :], gate_t[i][:, :], ACT.Sigmoid,
                                                 bias=consts[:, b:b + 1]).then_inc(gate_ready, 1)
                    elif kind == "branch_b" and step[3] == 1:
                        split_hi(G_B + SLOTS * step[1] + 2 + step[2] + SLOTS)

                def mix(pair, n=SLOTS):
                    for i in range(2):
                        m = 2 * pair + i
                        split_hi(G_A + 2 * i + SLOTS, pair, n)
                        act.wait_ge(out_read, O_A + 2 * i + 1 + n * pair)
                        b = 4 * DK
                        b_gate = consts[:, b + m:b + m + 1] if isinstance(m, int) else consts[:, bass.ds(m + b, 1)]
                        nc.scalar.activation(gate_t[i][:, :], gate_t[i][:, :], ACT.Sigmoid,
                                             bias=b_gate).then_inc(gate_ready, 1)
                        split_hi(G_A + 2 * i + 1 + SLOTS, pair, n)
                        act.wait_ge(mixed, m + 1)
                        copy(tile(m_hi, m), up_t[i][:, :]).then_inc(m_hi_ready, 1)

                with act.Fori(0, DK // 2 - 1) as pair:
                    mix(pair)
                mix(DK // 2 - 1)
                for m in range(DK):
                    act.wait_ge(out_read, O_OUT + m + 1)
                    copy(tile(h_hi, m), tile(xT, m), scale=gain(NORM_FFN2, m)).then_inc(h_hi_ready, 1)
                    split_hi(G_OUT + m + SLOTS)
                    square_free(NORM_FFN2, m)
                    square(tile(xT, m), m % 2, m == 0)

            for h in range(2):
                cols, blocks = slice(h * HALF, (h + 1) * HALF), slice(2 * h, 2 * h + 2)
                square_free(NORM_FINAL, DK - 1)
                act.wait_ge(last_updated, h + 1)
                nc.scalar.activation(sq[:, 1, cols], xT[:, (DK - 1) * SEQ + h * HALF:(DK - 1) * SEQ + (h + 1) * HALF],
                                     ACT.Square).then_inc(last_squared, 1)
                act.wait_ge(y_turned, DK + h)
                copy(y_rows[:, blocks, (DK - 1) * P:DK * P],
                     banks[7][:, cols].rearrange("p (t d) -> p t d", t=2)).then_inc(y_rows_ready, 1)
                act.wait_ge(rinv_ready, NORM_FINAL + 1 + h)
                act.wait_ge(y_rows_ready, DK + h)
                t = 2 * h + 1
                for c in range(2):
                    part = y_rows[:, t, c * D_MODEL // 2:(c + 1) * D_MODEL // 2]
                    copy(part, part, scale=rinv[:, t:t + 1]).then_inc(scaled_act, 1)

        @block.vector
        def _(dve):
            vec = nc.vector

            def split_lo(g, it=0, n=0):
                s = g % SLOTS
                nk = granule_tiles(g + n * it if isinstance(it, int) else g)
                dve.wait_ge(w_hi_ready, g + 1 + n * it)
                vec.tensor_tensor(w_lo[:, s, 0:nk, :], raw[:, s, 0:nk, :], w_hi[:, s, 0:nk, :].bitcast(F32),
                                  ALU.subtract).then_inc(w_lo_ready, 1)

            def lo(dst, full, hi):
                return vec.tensor_tensor(dst, full, hi.bitcast(F32), ALU.subtract)

            def new_h_lo(n, m):
                dve.wait_ge(h_hi_ready, m + (DK * n + 1))
                vec.scalar_tensor_tensor(out=tile(h_lo, m), in0=tile(xT, m), scalar=gain(n, m),
                                         in1=tile(h_hi, m).bitcast(F32), op0=ALU.mult,
                                         op1=ALU.subtract).then_inc(h_lo_ready, 1)

            def norm_factors(n):
                mean(n)
                dve.wait_ge(rinv_ready, n + 1)
                for t in range(TB):
                    last = vec.tensor_scalar(gb_t[:, t * P:(t + 1) * P], ident[:, :], rinv[:, t:t + 1], None, ALU.mult)
                last.then_inc(diag_ready, 1)
                dve.wait_ge(rstd_done, n + 1)
                vec.tensor_copy(rstd[:, :], banks[B_RSTD][:, :]).then_inc(rstd_ready, 1)
                dve.wait_ge(rstd_ready, n + 1)

            def mean(n, blocks=(0, TB), nth=0):
                t0, t1 = blocks
                dve.wait_ge(sum_done, n + 1 + nth)
                vec.tensor_scalar(var[:, t0:t1], banks[B_SUM][:, 2 * t0:2 * t1:2], 1.0 / D_MODEL, EPS, ALU.mult,
                                  ALU.add).then_inc(var_ready, 1)

            dve.wait_ge(gain_turned, 1)
            vec.tensor_copy(consts[:, 0:DK], banks[0][:, 0:DK]).then_inc(gain_ready, 1)
            dve.wait_ge(gain_ready, 1)
            for piece in X_ORDER:
                m = piece[1]
                if piece[0] == "h":
                    dve.wait_ge(h_hi_ready, m + 1)
                    vec.scalar_tensor_tensor(out=tile(h_lo, m), in0=banks[x_bank(m)][:, :], scalar=gain(NORM_FFN1, m),
                                             in1=tile(h_hi, m).bitcast(F32), op0=ALU.mult,
                                             op1=ALU.subtract).then_inc(h_lo_ready, 1)
                elif piece[0] == "x":
                    vec.tensor_copy(tile(xT, m), banks[x_bank(m)][:, :]).then_inc(x_ready, 1)
                elif piece[0] == "w":
                    split_lo(m)
            def ffn_up(r, it, first=False, n=SLOTS):
                for j in range(2):
                    g, o, f = G_UP[r] + 2 * j, O_UP[r] + 2 * j, FK * r + j
                    split_lo(g + SLOTS, it, n)
                    if first and j == 0:
                        norm_factors(NORM_FFN1 if r == 0 else NORM_FFN2)
                    dve.wait_ge(w_used, g + 1 + n * it)
                    vec.tensor_tensor(gate_t[j][:, :], banks[o % BANKS][:, :], rstd[:, :], ALU.mult).then_inc(out_read, 1)
                    split_lo(g + 1 + SLOTS, it, n)
                    dve.wait_ge(w_used, g + 2 + n * it)
                    vec.tensor_tensor(up_t[j][:, :], banks[(o + 1) % BANKS][:, :], rstd[:, :], ALU.mult).then_inc(out_read, 1)
                    dve.wait_ge(out_read, o + 2 + n * it)
                    dve.wait_ge(silu_ready, f + 1 + 2 * it)
                    vec.tensor_tensor(up_t[j][:, :], gate_t[j][:, :], up_t[j][:, :], ALU.mult).then_inc(product_ready, 1)
                    dve.wait_ge(a_hi_ready, f + 1 + 2 * it)
                    lo(tile(a_lo, 2 * it + j), up_t[j][:, :], tile(a_hi, 2 * it + j)).then_inc(a_lo_ready, 1)

            def residual(n, m, o, scale, it=0, per=0):
                vec.scalar_tensor_tensor(out=tile(xT, m), in0=banks[o % BANKS][:, :], scalar=scale, in1=tile(xT, m),
                                         op0=ALU.mult, op1=ALU.add).then_inc(out_read, 1)

            def ffn_down(r, it, last=False, n=2 * SLOTS):
                nrm = NORM_MIX if r == 0 else NORM_FINAL
                for j in range(2):
                    g, o, m = G_DOWN[r] + SLOTS * j, O_DOWN[r] + j, 2 * it + j
                    ahead = not (r == 1 and last and j == 1)
                    if not ahead:
                        break
                    for i in range(3):
                        split_lo(g + SLOTS + i, it, n)
                    dve.wait_ge(w_used, g + SLOTS + n * it)
                    residual(nrm, m, o, 0.5)
                    if nrm < NORM_FINAL:
                        dve.wait_ge(out_read, o + 1 + 2 * it)
                        new_h_lo(nrm, m)
                    split_lo(g + SLOTS + 3, it, n)

            for r in range(2):
                ffn_up(r, 0, first=True)
                if r == 0:
                    dve.wait_ge(consts_turned, 1)
                    vec.tensor_copy(consts[:, DK:ROWS], banks[6][:, 0:ROWS - DK]).then_inc(consts_ready, 1)
                    dve.wait_ge(fills_ready, 3)
                    dve.wait_ge(bias_done, 1)
                    vec.tensor_copy(bias_row[:, P - 1:P - 1 + NREL], banks[7][0:N_HEADS, 0:NREL]).then_inc(row_ready, 1)
                with dve.Fori(1, FK // 2 - 1) as it:
                    ffn_up(r, it)
                ffn_up(r, FK // 2 - 1)
                with dve.Fori(0, DK // 2 - 1) as it:
                    ffn_down(r, it)
                ffn_down(r, DK // 2 - 1, last=True)
                if r == 1:
                    break

                for step in steps:
                    kind = step[0]
                    if kind == "f":
                        grp = step[1]
                        split_lo(G_F + grp + SLOTS)
                        if grp == 0:
                            norm_factors(NORM_MIX)
                        dve.wait_ge(w_used, G_F + grp + 1)
                        vec.tensor_tensor(gate_t[grp % 2][:, :], banks[(O_F + grp) % BANKS][:, :], rstd[:, :],
                                          ALU.mult).then_inc(out_read, 1)
                        dve.wait_ge(proj_hi_ready, grp + 1)
                        lo(fy_lo[:, grp, :], gate_t[grp % 2][:, :], fy_hi[:, grp, :]).then_inc(proj_lo_ready, 1)
                        if grp == 1:
                            dve.wait_ge(tab_hi_ready, 1)
                            lo(tab_lo[:, :], tab_raw[:, :], tab_hi[:, :]).then_inc(tab_lo_ready, 1)
                    elif kind == "k":
                        split_lo(G_K + SLOTS)
                        dve.wait_ge(w_used, G_K + 1)
                        vec.tensor_tensor(ga_t[:, :], banks[O_K % BANKS][:, :], rstd[:, :], ALU.mult).then_inc(out_read, 1)
                        dve.wait_ge(proj_hi_ready, N_FGROUPS + 1)
                        for v in range(N_KV):
                            rows_v = slice(v * HD, (v + 1) * HD)
                            last = lo(kp_lo[rows_v, v, :], ga_t[rows_v, :], kp_hi[rows_v, v, :])
                        last.then_inc(proj_lo_ready, 1)
                    elif kind == "v":
                        split_lo(G_V + SLOTS)
                        dve.wait_ge(w_used, G_V + 1)
                        vec.tensor_tensor(ua_t[:, :], banks[O_V % BANKS][:, :], rstd[:, :], ALU.mult).then_inc(out_read, 1)
                    elif kind == "q":
                        c = step[1]
                        split_lo(G_Q + c + SLOTS)
                        dve.wait_ge(w_used, G_Q + c + 1)
                        q_t = gate_t[(c + 1) % 2]
                        vec.scalar_tensor_tensor(out=q_t[:, :], in0=banks[(O_Q + c) % BANKS][:, :], scalar=HD ** -0.5,
                                                 in1=rstd[:, :], op0=ALU.mult, op1=ALU.mult).then_inc(out_read, 1)
                        dve.wait_ge(proj_hi_ready, N_FGROUPS + 2 + c)
                        lo(qo_lo[:, c, :], q_t[:, :], qo_hi[:, c, :]).then_inc(proj_lo_ready, 1)
                    elif kind == "turn_v":
                        dve.wait_ge(v_hi_ready, 1)
                        lo(v_lo[:, :, :], banks[B_CH][:, :].rearrange("p (t d) -> p t d", t=TB),
                           v_hi[:, :, :]).then_inc(v_lo_ready, 1)
                    elif kind == "channels":
                        grp = step[1]
                        for i in range(2):
                            dve.wait_ge(ab_hi_ready, 2 * grp + i + 1)
                            lo(ab_lo[:, 2 * i:2 * i + 2, :],
                               banks[B_CH + i][:, :].rearrange("p (t d) -> p t d", t=2),
                               ab_hi[:, 2 * i:2 * i + 2, :]).then_inc(ab_lo_ready, 1)
                    elif kind == "positions":
                        grp, h = step[1], SEQ // 2
                        dve.wait_ge(odd_done, grp + 1)
                        dve.wait_ge(even_copied, grp + 1)
                        vec.tensor_tensor(y_t[:, 0:h + 1], even_t[:, 0:h + 1], banks[B_POS + 1][:, 0:h + 1],
                                          ALU.add).then_inc(y_ready, 1)
                        vec.tensor_tensor(y_t[:, SEQ - 1:h:-1], even_t[:, 1:h], banks[B_POS + 1][:, 1:h],
                                          ALU.subtract).then_inc(y_ready, 1)
                        dve.wait_ge(y_hi_ready, grp + 1)
                        lo(fy_lo[:, grp, :], y_t[:, :], fy_hi[:, grp, :]).then_inc(y_lo_ready, 1)
                    elif kind == "scores":
                        u, c = step[1:]
                        nb, kv, b = u // N_KV, u % N_KV, u % 2
                        blocks, w0 = window(nb)
                        width = len(blocks) * BLK
                        if u == 0 and c == 0:
                            dve.wait_ge(bias_landed, 16)
                            dve.wait_ge(sink_landed, 16)
                        dve.wait_ge(s_done, GQ * u + c + 1)
                        vec.tensor_tensor_reduce(
                            out=s_t[b][:, c, 0:width], in0=banks[B_S + c % 2][:, 0:width],
                            in1=bias[:, GQ * kv + c, w0 * BLK:w0 * BLK + width], scale=1.0, scalar=NEG,
                            op0=ALU.add, op1=ALU.max, accum_out=mx[:, b, c:c + 1]).then_inc(s_read, 1)
                    elif kind == "max":
                        u = step[1]
                        b, kv = u % 2, u % N_KV
                        sk = sink[:, GQ * kv:GQ * (kv + 1)]
                        dve.wait_ge(s_read, GQ * (u + 1))
                        vec.tensor_tensor(mx[:, b, :], mx[:, b, :], sk, ALU.max).then_inc(max_ready, 1)
                        dve.wait_ge(max_ready, 3 * u + 1)
                        vec.tensor_scalar(negm[:, b, :], mx[:, b, :], -1.0, None, ALU.mult).then_inc(max_ready, 1)
                        vec.tensor_tensor(sdiff[:, b, :], sk, mx[:, b, :], ALU.subtract).then_inc(max_ready, 1)
                    elif kind == "normalize":
                        u = step[1]
                        b = u % 2
                        width = len(window(u // N_KV)[0]) * BLK
                        dve.wait_ge(exp_ready, u + 1)
                        vec.tensor_tensor(den[:, b, :], psumr[:, b, :], esink[:, b, :], ALU.add).then_inc(den_ready, 1)
                        dve.wait_ge(den_ready, 2 * u + 1)
                        vec.reciprocal(rden[:, b, :], den[:, b, :]).then_inc(den_ready, 1)
                        dve.wait_ge(den_ready, 2 * u + 2)
                        for c in range(GQ):
                            sc = s_t[b][:, c, 0:width]
                            last = vec.tensor_scalar(sc, sc, rden[:, b, c:c + 1], None, ALU.mult)
                        last.then_inc(probs_ready, 1)
                    elif kind == "turn":
                        t = turn_index(*step[1:])
                        dve.wait_ge(pt_hi_ready, t + 1)
                        lo(pt_lo[:, t % 2, :], banks[B_PT[t % 2]][:, :], pt_hi[:, t % 2, :]).then_inc(pt_lo_ready, 1)
                    elif kind == "values":
                        u, b = step[1:]
                        nb, kv = u // N_KV, u % N_KV
                        if b == len(window(nb)[0]) - 1:
                            rows_v, cols = slice(kv * HD, (kv + 1) * HD), slice(nb * BLK, (nb + 1) * BLK)
                            dve.wait_ge(o_hi_ready, u + 1)
                            lo(qo_lo[rows_v, :, cols],
                               banks[B_O][rows_v, :].rearrange("p (c q) -> p c q", c=GQ),
                               qo_hi[rows_v, :, cols]).then_inc(o_lo_ready, 1)
                    elif kind == "gate_b" and step[3] == 3:
                        g, i = G_B + SLOTS * step[1] + step[2], step[2]
                        split_lo(g + SLOTS)
                        dve.wait_ge(w_used, g + 1)
                        bank = banks[B_B[(g - G_B) % 3]]
                        if step[1]:
                            dve.wait_ge(out_read, O_B + g - G_B - 1)
                        vec.tensor_tensor(gate_t[i][:, :], bank[:, :], rstd[:, :], ALU.mult).then_inc(out_read, 1)
                    elif kind == "branch_b" and step[3] == 1:
                        pair, i = step[1:3]
                        split_lo(G_B + SLOTS * pair + 2 + i + SLOTS)
                    elif kind == "take_b":
                        pair, i = step[1:]
                        dve.wait_ge(w_used, G_B + SLOTS * pair + 2 + i + 1)
                        dve.wait_ge(gate_ready, 2 * pair + i + 1)
                        bank = banks[B_B[(SLOTS * pair + 2 + i) % 3]]
                        vec.tensor_tensor(tile(mix_b, 2 * pair + i), bank[:, :], gate_t[i][:, :],
                                          ALU.mult).then_inc(out_read, 1)

                def mix(pair, n=SLOTS):
                    for i in range(2):
                        m, g, o = 2 * pair + i, G_A + 2 * i, O_A + 2 * i
                        split_lo(g + SLOTS, pair, n)
                        dve.wait_ge(out_read, o - 1 + n * pair)
                        dve.wait_ge(w_used, g + 1 + n * pair)
                        vec.tensor_tensor(gate_t[i][:, :], banks[o % BANKS][:, :], rstd[:, :], ALU.mult).then_inc(out_read, 1)
                        dve.wait_ge(gate_ready, m + (DK + 1))
                        dve.wait_ge(w_used, g + 2 + n * pair)
                        vec.tensor_tensor(up_t[i][:, :], banks[(o + 1) % BANKS][:, :], gate_t[i][:, :],
                                          ALU.mult).then_inc(out_read, 1)
                        dve.wait_ge(out_read, o + 2 + n * pair)
                        vec.tensor_tensor(up_t[i][:, :], up_t[i][:, :], tile(mix_b, m), ALU.add).then_inc(mixed, 1)
                        dve.wait_ge(m_hi_ready, m + 1)
                        lo(tile(m_lo, m), up_t[i][:, :], tile(m_hi, m)).then_inc(m_lo_ready, 1)
                        split_lo(g + 1 + SLOTS, pair, n)

                with dve.Fori(0, DK // 2 - 1) as pair:
                    mix(pair)
                mix(DK // 2 - 1)
                for m in range(DK):
                    dve.wait_ge(w_used, G_OUT + m + 1)
                    residual(NORM_FFN2, m, O_OUT + m, 1.0)
                    dve.wait_ge(out_read, O_OUT + m + 1)
                    new_h_lo(NORM_FFN2, m)
                    split_lo(G_OUT + m + SLOTS)

            for h in range(2):
                tail = slice((DK - 1) * SEQ + h * HALF, (DK - 1) * SEQ + (h + 1) * HALF)
                cols = slice(h * HALF, (h + 1) * HALF)
                dve.wait_ge(last_done, h + 1)
                vec.scalar_tensor_tensor(out=xT[:, tail], in0=banks[last_bank(h)][:, cols], scalar=0.5, in1=xT[:, tail],
                                         op0=ALU.mult, op1=ALU.add).then_inc(last_updated, 1)
                dve.wait_ge(last_updated, h + 1)
                vec.tensor_scalar(gate_t[1][:, cols], xT[:, tail], gain(NORM_FINAL, DK - 1), None,
                                  ALU.mult).then_inc(last_scaled, 1)
                mean(NORM_FINAL, (2 * h, 2 * h + 2), h)
                dve.wait_ge(rinv_ready, NORM_FINAL + 1 + h)
                dve.wait_ge(y_rows_ready, DK + h)
                t = 2 * h
                for c in range(2):
                    part = y_rows[:, t, c * D_MODEL // 2:(c + 1) * D_MODEL // 2]
                    vec.tensor_scalar(part, part, rinv[:, t:t + 1], None, ALU.mult).then_inc(scaled_dve, 1)

        @block.gpsimd
        def _(pool):
            nc.gpsimd.memset(ident[:, :], 0.0).then_inc(ident_ready, 1)
            pool.wait_ge(ident_ready, 1)
            nc.gpsimd.affine_select(out=ident[:, :], in_=ident[:, :], compare_op=ALU.not_equal, fill=1.0, base=0,
                                    pattern=[[-1, P]], channel_multiplier=1).then_inc(ident_ready, 1)
            nc.gpsimd.memset(ones[:, :], 1.0).then_inc(fills_ready, 1)
            nc.gpsimd.memset(half[:, :], -0.5).then_inc(fills_ready, 1)
            nc.gpsimd.memset(bias_row[:, :], NEG).then_inc(fills_ready, 1)
            pool.wait_ge(fills_ready, 3)
            for n in range(4):
                for m in range(1, DK - 1 if n == NORM_FINAL else DK):
                    pool.wait_ge(sq_ready, DK * n + m + 1)
                    if m > 1:
                        pool.wait_ge(sum_added, (DK - 1) * n + m - 1)
                    nc.gpsimd.tensor_tensor(ssum[:, :], ssum[:, :], sq[:, m % 2, :], ALU.add).then_inc(sum_added, 1)
                for i in range(2 if n == NORM_FINAL else 1):
                    blocks = slice(2 * i, 2 * i + 2) if n == NORM_FINAL else slice(0, TB)
                    pool.wait_ge(var_ready, n + 1 + i)
                    nc.gpsimd.tensor_tensor(rinv[:, blocks], var[:, blocks], half[:, blocks],
                                            ALU.pow).then_inc(rinv_ready, 1)
                if n == NORM_MIX:
                    pool.wait_ge(rinv_ready, n + 1)
                    nc.gpsimd.memset(kp_hi[:, :, :].bitcast(F32), 0.0).then_inc(zeros_ready, 1)
                    nc.gpsimd.memset(kp_lo[:, :, :].bitcast(F32), 0.0).then_inc(zeros_ready, 1)

        @block.tensor
        def _(pe):
            def passes(out_ap, pairs, lo_ready=None, first=True, last=True):
                for i, (w, x_) in enumerate(pairs):
                    nc.tensor.matmul(out_ap, w[0], x_[0], start=first and i == 0, stop=False)
                    nc.tensor.matmul(out_ap, w[0], x_[1], start=False, stop=False)
                if lo_ready is not None:
                    pe.wait_ge(*lo_ready)
                for i, (w, x_) in enumerate(pairs):
                    mm = nc.tensor.matmul(out_ap, w[1], x_[0], start=False, stop=last and i == len(pairs) - 1)
                return mm

            def granule(g, out_ap, x_parts, first=True, last=True, it=0, n=0, tiles=None, x_ready_at=None, done=True,
                        by_tile=False,
                        between=None):
                s = g % SLOTS
                tiles = tiles if tiles is not None else range(granule_tiles(g))
                pe.wait_ge(w_hi_ready, g + 1 + n * it)
                for i, k in enumerate(tiles):
                    if between and by_tile:
                        between(k)
                    if x_ready_at:
                        x_ready_at(k)
                    xh, xl = x_parts(k)
                    nc.tensor.matmul(out_ap, w_hi[:, s, k, :], xh, start=first and i == 0, stop=False)
                    mm = nc.tensor.matmul(out_ap, w_hi[:, s, k, :], xl, start=False, stop=False)
                    if by_tile:
                        if i == 0:
                            pe.wait_ge(w_lo_ready, g + 1 + n * it)
                        mm = nc.tensor.matmul(out_ap, w_lo[:, s, k, :], xh, start=False,
                                              stop=last and i == len(tiles) - 1)
                if not by_tile:
                    if between:
                        between()
                    pe.wait_ge(w_lo_ready, g + 1 + n * it)
                for i, k in enumerate(() if by_tile else tiles):
                    mm = nc.tensor.matmul(out_ap, w_lo[:, s, k, :], x_parts(k)[0], start=False,
                                          stop=last and i == len(tiles) - 1)
                if done:
                    mm.then_inc(w_used, 1)
                return mm

            def h_parts(k):
                return tile(h_hi, k), tile(h_lo, k)

            def h_ready(n):
                def wait(k):
                    pe.wait_ge(h_hi_ready, DK * n + k + 1)
                    pe.wait_ge(h_lo_ready, DK * n + k + 1)
                return wait

            def sum_squares(n):
                pe.wait_ge(sum_added, (DK - 1) * (n + 1))
                if n == NORM_FFN1:
                    pe.wait_ge(x_ready, DK)
                for t in range(TB):
                    mm = nc.tensor.matmul(banks[B_SUM][:, 2 * t:2 * t + 2], ssum[:, t * P:(t + 1) * P], ones[:, 0:2],
                                          start=True, stop=True)
                mm.then_inc(sum_done, 1)

            def spread_factors(n):
                pe.wait_ge(diag_ready, n + 1)
                nc.tensor.matmul(banks[B_RSTD][:, :], ones[:, :], gb_t[:, :], start=True, stop=True).then_inc(rstd_done, 1)

            def x_tile(m):
                if m % 2 == 0:
                    pe.wait_ge(x_landed[m // 2], 16)
                if m >= X_BANKS:
                    pe.wait_ge(x_ready, m - X_BANKS + 1)
                for t in range(TB):
                    mm = nc.tensor.transpose(banks[x_bank(m)][:, t * P:(t + 1) * P],
                                             x_rows[:, t, m * P:(m + 1) * P], ident[:, :])
                mm.then_inc(turned, 1)

            def warm_up(count):
                for _ in range(count):
                    nc.tensor.matmul(banks[1][:, 0:P], ones[:, :], ones[:, :], start=True, stop=True)

            pe.wait_ge(fills_ready, 1)
            warm_up(6)
            pe.wait_ge(ident_ready, 2)
            pe.wait_ge(gain_landed, 16)
            nc.tensor.transpose(banks[0][:, 0:DK], gain_rows[:, :], ident[0:DK, 0:DK]).then_inc(gain_turned, 1)
            for m in range(X_BANKS):
                x_tile(m)

            def other_constants():
                pe.wait_ge(rows_landed, 16 * 4)
                nc.tensor.transpose(banks[6][:, 0:ROWS - DK], rows[0:ROWS - DK, 0:P], ident[0:ROWS - DK, 0:ROWS - DK]
                                    ).then_inc(consts_turned, 1)
                pe.wait_ge(buckets_landed, 32)
                nc.tensor.matmul(banks[7][0:N_HEADS, 0:NREL + 1], table_b[:, :], onehot[:, :], start=True,
                                 stop=True).then_inc(bias_done, 1)

            def x_rest(k):
                if k in (2, 4):
                    x_tile(X_BANKS + k // 2 - 1)

            def ffn_up(r, it, first=False, n=SLOTS):
                nrm = NORM_FFN1 if r == 0 else NORM_FFN2
                for j in range(SLOTS):
                    g, o = G_UP[r] + j, O_UP[r] + j
                    if not first or o - 3 > 0:
                        pe.wait_ge(out_read, o - 3 + n * it)
                    if first and r == 0 and j >= 2:
                        pe.wait_ge(x_ready, DK)
                    granule(g, banks[o % BANKS][:, :], h_parts, it=it, n=n, by_tile=first and j == 0,
                            x_ready_at=h_ready(nrm) if first and j == 0 else None,
                            between=x_rest if first and r == j == 0 else
                            (lambda: spread_factors(nrm)) if first and j == 3 else None)
                    if first and j == 2:
                        sum_squares(nrm)
                        if r == 0:
                            other_constants()

            def a_parts(at_):
                return lambda k: (tile(a_hi, at_ + k), tile(a_lo, at_ + k))

            def turn_rows(m, odd):
                pe.wait_ge(h_hi_ready, m + (DK * NORM_FINAL + 1))
                if not isinstance(m, int) or m >= 2:
                    pe.wait_ge(y_rows_ready, m - 1)
                for t in range(TB):
                    mm = nc.tensor.transpose(banks[6 + odd][:, t * P:(t + 1) * P],
                                             gate_t[odd][:, t * P:(t + 1) * P], ident[:, :])
                mm.then_inc(y_turned, 1)

            def ffn_down(r, it, first=False, last=False, n=2 * SLOTS):
                for c in range(2):
                    if last and c == 1:
                        break
                    o = O_DOWN[r] + c
                    pe.wait_ge(out_read, o - 1 + 2 * it)
                    for j in range(SLOTS):
                        g = G_DOWN[r] + SLOTS * c + j

                        def a_ready(k, at_=DOWN_AT[j]):
                            if k == 0 or at_ + k >= FK - 2:
                                need = FK * r + (at_ + k + 1 if at_ + k >= FK - 2 else FK - 2)
                                pe.wait_ge(a_hi_ready, need)
                                pe.wait_ge(a_lo_ready, need)

                        granule(g, banks[o % BANKS][:, :], a_parts(DOWN_AT[j]), first=j == 0, last=j == SLOTS - 1,
                                it=it, n=n, x_ready_at=a_ready if c == 0 and j in (0, SLOTS - 1) else None)
                        if r == 1 and j == 1 and not (first and c == 0):
                            turn_rows(2 * it + c - 1, 1 - c)

            for r in range(2):
                ffn_up(r, 0, first=True)
                with pe.Fori(1, FK // 2) as it:
                    ffn_up(r, it)
                ffn_down(r, 0, first=True)
                with pe.Fori(1, DK // 2 - r) as it:
                    ffn_down(r, it)
                if r == 1:
                    ffn_down(r, DK // 2 - 1, last=True)
                    break

                for step in steps:
                    kind = step[0]
                    if kind == "f":
                        grp = step[1]
                        o = O_F + grp
                        pe.wait_ge(out_read, o - 1 if grp < 2 else o - 3)
                        granule(G_F + grp, banks[o % BANKS][:, :], h_parts, by_tile=grp == 0,
                                x_ready_at=h_ready(NORM_MIX) if grp == 0 else None)
                        if grp == 0:
                            sum_squares(NORM_MIX)
                        if grp == 1:
                            spread_factors(NORM_MIX)
                    elif kind in ("k", "v", "q"):
                        i = {"k": 0, "v": 1, "q": 2}[kind] + (step[1] if kind == "q" else 0)
                        o = O_K + i
                        pe.wait_ge(out_read, o - 3)
                        granule(G_K + i, banks[o % BANKS][:, :], h_parts)
                    elif kind == "turn_v":
                        pe.wait_ge(out_read, O_V + 1)
                        pe.wait_ge(ab_lo_ready, 2 * N_FGROUPS)
                        for t in range(TB):
                            mm = nc.tensor.transpose(banks[B_CH][:, t * P:(t + 1) * P], ua_t[:, t * P:(t + 1) * P],
                                                     ident[:, :])
                        mm.then_inc(v_turned, 1)
                    elif kind == "channels":
                        grp = step[1]
                        pe.wait_ge(proj_lo_ready, grp + 1)
                        if grp == 0:
                            pe.wait_ge(tab_lo_ready, 1)
                        else:
                            pe.wait_ge(ab_lo_ready, 2 * grp)
                        ch = slice(CH_AT, CH_AT + 2 * FG_DIM)
                        for t in range(TB):
                            tok = slice(t * P, (t + 1) * P)
                            o_ap = banks[B_CH + t // 2][:, (t % 2) * 2 * FG_DIM:(t % 2 + 1) * 2 * FG_DIM]
                            mm = passes(o_ap, [((fy_hi[:, grp, tok], fy_lo[:, grp, tok]),
                                                (tab_hi[:, ch], tab_lo[:, ch]))])
                            if t % 2:
                                mm.then_inc(ab_done, 1)
                    elif kind == "positions":
                        grp = step[1]
                        pe.wait_ge(ab_lo_ready, 2 * grp + 2)
                        if grp:
                            pe.wait_ge(y_ready, 2 * grp)
                        for odd in range(2):
                            pairs = []
                            for t in range(TB):
                                c0 = slice(odd * FG_DIM, (odd + 1) * FG_DIM)
                                k0 = (2 * t + odd) * NPOS
                                pairs.append(((ab_hi[:, t, c0], ab_lo[:, t, c0]),
                                              (tab_hi[:, k0:k0 + NPOS], tab_lo[:, k0:k0 + NPOS])))
                            passes(banks[B_POS + odd][:, 0:NPOS], pairs).then_inc(odd_done if odd else even_done, 1)
                    elif kind == "scores":
                        u, c = step[1:]
                        nb, kv = u // N_KV, u % N_KV
                        blocks, _ = window(nb)
                        keys = slice(blocks[0] * BLK, (blocks[-1] + 1) * BLK)
                        q = slice(nb * BLK, (nb + 1) * BLK)
                        if u == 0:
                            pe.wait_ge(proj_lo_ready, N_FGROUPS + 2 + c)
                            pe.wait_ge(v_lo_ready, 1)
                        if GQ * u + c >= 2:
                            pe.wait_ge(s_read, GQ * u + c - 1)
                        passes(banks[B_S + c % 2][:, 0:len(blocks) * BLK],
                               [((qo_hi[:, c, q], qo_lo[:, c, q]), (kp_hi[:, kv, keys], kp_lo[:, kv, keys]))]
                               ).then_inc(s_done, 1)
                    elif kind == "turn":
                        u, b = step[1:]
                        t = turn_index(u, b)
                        pe.wait_ge(probs_ready, u + 1)
                        if t >= 2:
                            pe.wait_ge(pt_lo_ready, t - 1)
                        elif t == 0:
                            pe.wait_ge(out_read, O_Q + 1)
                            pe.wait_ge(y_ready, 2 * N_FGROUPS)
                        for c in range(GQ):
                            mm = nc.tensor.transpose(banks[B_PT[t % 2]][:, c * BLK:(c + 1) * BLK],
                                                     s_t[u % 2][:, c, b * BLK:(b + 1) * BLK], ident[:, :])
                        mm.then_inc(pt_done, 1)
                    elif kind == "values":
                        u, b = step[1:]
                        t = turn_index(u, b)
                        blocks, _ = window(u // N_KV)
                        blk = blocks[b]
                        if t == 0:
                            pe.wait_ge(out_read, O_Q + 2)
                        if b == 0 and u >= 1:
                            pe.wait_ge(o_lo_ready, u)
                        o_bank = banks[B_O][:, :]
                        pe.wait_ge(pt_hi_ready, t + 1)
                        nc.tensor.matmul(o_bank, v_hi[:, blk, :], pt_hi[:, t % 2, :], start=b == 0, stop=False)
                        nc.tensor.matmul(o_bank, v_lo[:, blk, :], pt_hi[:, t % 2, :], start=False, stop=False)
                        pe.wait_ge(pt_lo_ready, t + 1)
                        nc.tensor.matmul(o_bank, v_hi[:, blk, :], pt_lo[:, t % 2, :], start=False,
                                         stop=b == len(blocks) - 1).then_inc(pt_used, 1)
                    elif kind == "gate_b":
                        pair, i, quarter = step[1:]
                        n = SLOTS * pair + i
                        if quarter == 0:
                            if n == 0:
                                pe.wait_ge(y_ready, 2 * N_FGROUPS)
                            else:
                                pe.wait_ge(out_read, O_B + n - 2)
                        granule(G_B + n, banks[B_B[n % 3]][:, :], h_parts, first=quarter == 0, last=quarter == 3,
                                tiles=range(2 * quarter, 2 * quarter + 2), done=quarter == 3)
                    elif kind == "branch_b":
                        pair, i, half_ = step[1:]
                        n = SLOTS * pair + 2 + i
                        if half_ == 0:
                            pe.wait_ge(out_read, O_B + n - 2)
                            pe.wait_ge(y_lo_ready, N_FGROUPS)
                        granule(G_B + n, banks[B_B[n % 3]][:, :],
                                lambda k: (fy_hi[:, k, :], fy_lo[:, k, :]), first=half_ == 0, last=half_ == 1,
                                tiles=range(2 * half_, 2 * half_ + 2), done=half_ == 1)

                with pe.Fori(0, DK // 2) as pair:
                    pe.wait_ge(pt_lo_ready, turn_index(TB * N_KV, 0))
                    for j in range(SLOTS):
                        if j == 1:
                            pe.wait_ge(o_lo_ready, TB * N_KV)
                        o = O_A + j
                        pe.wait_ge(out_read, o - 3 + SLOTS * pair)
                        granule(G_A + j, banks[o % BANKS][:, :],
                                (lambda k: (qo_hi[:, k, :], qo_lo[:, k, :])) if j % 2 else h_parts,
                                it=pair, n=SLOTS)

                def mixed_ready(k):
                    if k == 0 or k == DK - 1:
                        need = DK - 1 if k == 0 else DK
                        pe.wait_ge(m_hi_ready, need)
                        pe.wait_ge(m_lo_ready, need)

                for j in range(DK):
                    o = O_OUT + j
                    pe.wait_ge(out_read, o - 3)
                    granule(G_OUT + j, banks[o % BANKS][:, :], lambda k: (tile(m_hi, k), tile(m_lo, k)),
                            x_ready_at=mixed_ready if j == 0 else None, by_tile=j == 0)

            def finish(h):
                pe.wait_ge(sum_added, (DK - 1) * (NORM_FINAL + 1) - 1)
                if h:
                    pe.wait_ge(var_ready, NORM_FINAL + 1)
                for last_one in (False, True):
                    if last_one:
                        pe.wait_ge(last_squared, h + 1)
                    for t in (2 * h, 2 * h + 1):
                        squares = sq[:, 1, t * P:(t + 1) * P] if last_one else ssum[:, t * P:(t + 1) * P]
                        mm = nc.tensor.matmul(banks[B_SUM][:, 2 * t:2 * t + 2], squares, ones[:, 0:2],
                                              start=not last_one and t == 2 * h, stop=last_one and t == 2 * h + 1)
                mm.then_inc(sum_done, 1)
                pe.wait_ge(last_scaled, h + 1)
                pe.wait_ge(y_rows_ready, DK - 2 + h)
                for t in (2 * h, 2 * h + 1):
                    mm = nc.tensor.transpose(banks[7][:, t * P:(t + 1) * P], gate_t[1][:, t * P:(t + 1) * P],
                                             ident[:, :])
                mm.then_inc(y_turned, 1)

            pe.wait_ge(out_read, O_DOWN[1] + DK - 2)
            for h in range(2):
                for j in range(SLOTS):
                    at_ = DOWN_AT[j]

                    def parts(k):
                        cols = slice((at_ + k) * SEQ + h * HALF, (at_ + k) * SEQ + (h + 1) * HALF)
                        return a_hi[:, cols], a_lo[:, cols]

                    mm = granule(G_END - SLOTS + j, banks[last_bank(h)][:, h * HALF:(h + 1) * HALF], parts,
                                 first=j == 0, last=j == SLOTS - 1, done=False)
                    if j == SLOTS - 1:
                        mm.then_inc(last_done, 1)
                    if h == 0 and j == 1:
                        turn_rows(DK - 2, 0)
                    if h == 1 and j == 1:
                        finish(0)
            finish(1)


INPUTS = ["x", "g_ffn1", "w_up1", "w_down1", "g_mix", "w_in", "b_gate", "sink", "rel_bias", "w_branch_a",
          "w_branch_b", "w_out", "g_ffn2", "w_up2", "w_down2", "g_final"]


def kernel(**inputs):
    import concourse.bacc as bacc
    from concourse.bass_utils import run_bass_kernel_spmd

    nc = bacc.Bacc("TRN2", target_bir_lowering=False, num_devices=1)
    arrays, io = {}, {}
    host = {name: np.ascontiguousarray(inputs[name]) for name in INPUTS}
    host.update(shape_constants())
    for name, a in host.items():
        arrays[f"in_{name}_dram"] = a
        io[name] = nc.dram_tensor(f"in_{name}_dram", a.shape, mybir.dt.from_np(a.dtype), kind="ExternalInput").ap()
    io["out"] = nc.dram_tensor("out_dram", (1, SEQ, D_MODEL), F32, kind="ExternalOutput").ap()
    build(nc, io)
    r = run_bass_kernel_spmd(nc, [arrays], core_ids=[0])
    return r.results[0]["out_dram"]
```
